# Optimizing a Trainium2 kernel written in Bass

```python
import math
import jax
import jax.numpy as jnp
from jax import lax
import numpy as np

D_MODEL = 1024
BATCH = 1
SEQ = 256
DEPTH = 2

GRID_W = 64
CTX_LEN = 256
EPS = 1e-6
F32 = jnp.float32
HEAD_DIM = 64
ATT_WIDTH = D_MODEL // 2
ATT_HEADS = ATT_WIDTH // HEAD_DIM
ATT_KV_HEADS = ATT_HEADS // 4
ATT_GROUP = ATT_HEADS // ATT_KV_HEADS
WINDOW = 128
ATT_BLOCK = 128
ROPE_THETA = 10000.0
ROPE_AXIS_DIM = HEAD_DIM // 2
SSD_WIDTH = D_MODEL // 4
SSD_HEAD_DIM = 64
SSD_HEADS = SSD_WIDTH // SSD_HEAD_DIM
SSD_STATE = 64
SSD_GROUPS = 2
SSD_CONV = 3
SSD_CHUNK = 128
HYENA_WIDTH = D_MODEL // 4
HYENA_GROUPS = 4
HYENA_ORDER = 2
HYENA_CONV = 3
HYENA_POS_DIM = 33
HYENA_FILTER_HIDDEN = 64
HYENA_FAST_DECAY = 0.3
HYENA_SLOW_DECAY = 1.5
HYENA_DECAY_TARGET = 1e-2
MIX_WIDTH = ATT_WIDTH + SSD_WIDTH + HYENA_WIDTH
Q_COLS = ATT_HEADS * HEAD_DIM
KV_COLS = ATT_KV_HEADS * HEAD_DIM
SSD_XBC_COLS = SSD_WIDTH + 2 * SSD_GROUPS * SSD_STATE
SSD_DT_COLS = 2 * SSD_HEADS
HY_COLS = (HYENA_ORDER + 1) * HYENA_WIDTH
PROJ_WIDTH = Q_COLS + 2 * KV_COLS + SSD_WIDTH + SSD_XBC_COLS + SSD_DT_COLS + HY_COLS
FFN_DIM = 256 * ((8 * D_MODEL // 3 + 255) // 256)
N_EXPERTS = 8
MOE_TOP_K = 2
EXPERT_DIM = FFN_DIM

kernel_name = 'hybrid_swa_ssd_hyena_moe_dit'

def _rms(x):
    xf = x.astype(F32)
    return (xf * lax.rsqrt(jnp.mean(xf * xf, axis=-1, keepdims=True) + EPS)).astype(x.dtype)

def rms_norm(x, g):
    return _rms(x) * g

def group_rms_norm(x, g, groups):
    shp = x.shape
    return _rms(x.reshape(shp[:-1] + (groups, shp[-1] // groups))).reshape(shp) * g

def short_conv(u, w, b):
    k = w.shape[0]
    y = lax.conv_general_dilated(u, w[:, None, :], window_strides=(1,), padding=[(k // 2, k // 2)],
                                 dimension_numbers=('NWC', 'WIO', 'NWC'), feature_group_count=u.shape[-1])
    return y + b

def swiglu(t, wg, wu, wd):
    return (jax.nn.silu(t @ wg) * (t @ wu)) @ wd

def moe_swiglu(h, router, wg, wu, wd):
    shp = h.shape
    t = h.reshape(-1, shp[-1])
    logits = (t @ router).astype(F32)
    top_v, top_i = lax.top_k(logits, MOE_TOP_K)
    top_w = jax.nn.softmax(top_v, axis=-1)
    combine = jnp.sum(jax.nn.one_hot(top_i, N_EXPERTS, dtype=F32) * top_w[..., None], axis=1).astype(h.dtype)
    out = jnp.zeros_like(t)
    for e in range(N_EXPERTS):
        out = out + combine[:, e:e + 1] * swiglu(t, wg[e], wu[e], wd[e])
    return out.reshape(shp)

def channel_mixer(h, layer, ffn_w_gate, ffn_w_up, ffn_w_down, moe_router, moe_w_gate, moe_w_up, moe_w_down):
    j = layer // 2
    if layer % 2 == 0:
        return swiglu(h, ffn_w_gate[j], ffn_w_up[j], ffn_w_down[j])
    return moe_swiglu(h, moe_router[j], moe_w_gate[j], moe_w_up[j], moe_w_down[j])

def axial_rope_tables(seq_len):
    rows = seq_len // GRID_W
    row = jnp.repeat(jnp.arange(rows, dtype=F32), GRID_W)
    col = jnp.tile(jnp.arange(GRID_W, dtype=F32), rows)
    inv = ROPE_THETA ** (-jnp.arange(0, ROPE_AXIS_DIM, 2, dtype=F32) / ROPE_AXIS_DIM)
    ang = jnp.stack([row[:, None] * inv, col[:, None] * inv], axis=1)
    return jnp.cos(ang), jnp.sin(ang)

def apply_axial_rope(x, cos, sin):
    xr = x.reshape(x.shape[:-1] + (2, 2, ROPE_AXIS_DIM // 2))
    x1, x2 = xr[..., 0, :], xr[..., 1, :]
    cs = cos[None, :, None].astype(x.dtype)
    sn = sin[None, :, None].astype(x.dtype)
    return jnp.stack([x1 * cs - x2 * sn, x1 * sn + x2 * cs], axis=-2).reshape(x.shape)

def _heads(t, n):
    return t.reshape(t.shape[:-1] + (n, HEAD_DIM))

def latent_window_attention(q, k, v, k_ctx, v_ctx, sink):
    b, seq_len = q.shape[:2]
    band = ATT_BLOCK + 2 * WINDOW
    pad = ((0, 0), (WINDOW, WINDOW), (0, 0), (0, 0))
    kp = jnp.pad(k, pad)
    vp = jnp.pad(v, pad)
    rel = jnp.arange(band)[None, :] - WINDOW - jnp.arange(ATT_BLOCK)[:, None]

    def one_block(i):
        start = i * ATT_BLOCK
        qb = lax.dynamic_slice_in_dim(q, start, ATT_BLOCK, axis=1)
        kb = lax.dynamic_slice_in_dim(kp, start, band, axis=1)
        vb = lax.dynamic_slice_in_dim(vp, start, band, axis=1)
        kpos = start - WINDOW + jnp.arange(band)
        valid = (jnp.abs(rel) <= WINDOW) & ((kpos >= 0) & (kpos < seq_len))[None, :]
        s_loc = jnp.where(valid, jnp.einsum('bqhgd,bkhd->bhgqk', qb, kb).astype(F32), -jnp.inf)
        s_ctx = jnp.einsum('bqhgd,bkhd->bhgqk', qb, k_ctx).astype(F32)
        s_snk = jnp.broadcast_to(sink[None, :, :, None, None], s_ctx.shape[:-1] + (1,))
        p = jax.nn.softmax(jnp.concatenate([s_loc, s_ctx, s_snk], axis=-1), axis=-1).astype(v.dtype)
        return (jnp.einsum('bhgqk,bkhd->bqhgd', p[..., :band], vb)
                + jnp.einsum('bhgqk,bkhd->bqhgd', p[..., band:-1], v_ctx))

    out = lax.map(one_block, jnp.arange(seq_len // ATT_BLOCK))
    return jnp.moveaxis(out, 0, 1).reshape(b, seq_len, ATT_WIDTH)

def context_attention(q, k, v, sink):
    b, ctx_len = q.shape[:2]
    s = jnp.einsum('bqhgd,bkhd->bhgqk', q, k).astype(F32)
    s_snk = jnp.broadcast_to(sink[None, :, :, None, None], s.shape[:-1] + (1,))
    p = jax.nn.softmax(jnp.concatenate([s, s_snk], axis=-1), axis=-1).astype(v.dtype)
    return jnp.einsum('bhgqk,bkhd->bqhgd', p[..., :-1], v).reshape(b, ctx_len, ATT_WIDTH)

def ssd_prep(xbc, dt_raw, lp):
    xbc = jax.nn.silu(short_conv(xbc, lp['ssd_conv_w'], lp['ssd_conv_b']))
    xs, bm, cm = jnp.split(xbc, [SSD_WIDTH, SSD_WIDTH + SSD_GROUPS * SSD_STATE], axis=-1)
    b, seq_len = xs.shape[:2]
    rep = SSD_HEADS // SSD_GROUPS
    bh = jnp.repeat(bm.reshape(b, seq_len, SSD_GROUPS, SSD_STATE), rep, axis=2)
    ch = jnp.repeat(cm.reshape(b, seq_len, SSD_GROUPS, SSD_STATE), rep, axis=2)
    dt = jax.nn.softplus(dt_raw.astype(F32).reshape(b, seq_len, 2, SSD_HEADS) + lp['ssd_dt_bias'].astype(F32))
    return xs.reshape(b, seq_len, SSD_HEADS, SSD_HEAD_DIM), bh, ch, dt

def ssd_chunked(xh, dt, a, bh, ch, h0, want_y):
    b, seq_len, nh, hp = xh.shape
    nc = seq_len // SSD_CHUNK
    shp = (b, nc, SSD_CHUNK)
    xdt = (xh.astype(F32) * dt[..., None]).reshape(shp + (nh, hp))
    bc = bh.astype(F32).reshape(shp + (nh, SSD_STATE))
    la = jnp.cumsum((dt * a).reshape(shp + (nh,)), axis=2)
    w_end = jnp.exp(la[:, :, -1:] - la)
    states = jnp.einsum('bcshn,bcshp->bchpn', bc, xdt * w_end[..., None])

    def step(h, inp):
        s, dec = inp
        return h * dec[:, :, None, None] + s, h

    h_last, h_start = lax.scan(step, h0, (jnp.moveaxis(states, 1, 0), jnp.moveaxis(jnp.exp(la[:, :, -1]), 1, 0)))
    if not want_y:
        return None, h_last
    cc = ch.astype(F32).reshape(shp + (nh, SSD_STATE))
    seg = la[:, :, :, None] - la[:, :, None, :]
    lower = jnp.tril(jnp.ones((SSD_CHUNK, SSD_CHUNK), bool))[None, None, :, :, None]
    decay = jnp.exp(jnp.where(lower, seg, -jnp.inf))
    scores = jnp.einsum('bclhn,bcshn->bclsh', cc, bc)
    y_diag = jnp.einsum('bclsh,bcshp->bclhp', scores * decay, xdt)
    y_off = jnp.einsum('bclhn,bchpn->bclhp', cc, jnp.moveaxis(h_start, 0, 1)) * jnp.exp(la)[..., None]
    return (y_diag + y_off).reshape(b, seq_len, nh, hp), h_last

def _flip(t, rev):
    return jnp.flip(t, axis=1) if rev else t

def ssd_bidirectional(lat, ctx, a_log, d_skip, want_ctx):
    a = -jnp.exp(a_log.astype(F32))
    xl, bl, cl, dl = lat
    xc, bc, cc, dc = ctx
    h0 = jnp.zeros((xl.shape[0], SSD_HEADS, SSD_HEAD_DIM, SSD_STATE), F32)
    dsk = d_skip.astype(F32)[:, None]
    y_lat = xl.astype(F32) * dsk
    y_ctx = xc.astype(F32) * dsk if want_ctx else None
    for direction in range(2):
        rev = direction == 1
        yc, hc = ssd_chunked(_flip(xc, rev), _flip(dc[:, :, direction], rev), a[direction],
                             _flip(bc, rev), _flip(cc, rev), h0, want_ctx)
        yl, _ = ssd_chunked(_flip(xl, rev), _flip(dl[:, :, direction], rev), a[direction],
                            _flip(bl, rev), _flip(cl, rev), hc, True)
        y_lat = y_lat + _flip(yl, rev)
        if want_ctx:
            y_ctx = y_ctx + _flip(yc, rev)
    return y_lat, y_ctx

def hyena_filters(seq_len, lp):
    t = jnp.linspace(0.0, 1.0, seq_len, dtype=F32)[:, None]
    w = (2.0 * math.pi / seq_len) * jnp.arange(seq_len, dtype=F32)[:, None]
    bands = (HYENA_POS_DIM - 1) // 2
    freqs = jnp.linspace(1e-4, bands - 1, bands, dtype=F32)[None, :]
    z = jnp.concatenate([t, jnp.cos(freqs * w), -jnp.sin(freqs * w)], axis=-1)
    h = jnp.sin(lp['hy_f1'].astype(F32) * (z @ lp['hy_w1'].astype(F32) + lp['hy_b1'].astype(F32)))
    h = jnp.sin(lp['hy_f2'].astype(F32) * (h @ lp['hy_w2'].astype(F32) + lp['hy_b2'].astype(F32)))
    h = (h @ lp['hy_w3'].astype(F32)).reshape(seq_len, 2, HYENA_ORDER, HYENA_WIDTH)
    deltas = jnp.abs(jnp.linspace(math.log(HYENA_DECAY_TARGET) / HYENA_SLOW_DECAY,
                                  math.log(HYENA_DECAY_TARGET) / HYENA_FAST_DECAY, HYENA_WIDTH, dtype=F32))
    h = h * jnp.exp(-t * deltas)[:, None, None, :]
    k2 = jnp.concatenate([h[:, 0], jnp.zeros((1, HYENA_ORDER, HYENA_WIDTH), F32),
                          jnp.flip(h[1:, 1], axis=0)], axis=0)
    return jnp.fft.rfft(k2, axis=0)

def long_conv(u, kf, bias):
    seq_len = u.shape[1]
    uf = u.astype(F32)
    y = jnp.fft.irfft(jnp.fft.rfft(uf, n=2 * seq_len, axis=1) * kf[None], n=2 * seq_len, axis=1)[:, :seq_len]
    return (y + uf * bias.astype(F32)).astype(u.dtype)

def hyena_operator(u, lp):
    kf = hyena_filters(u.shape[1], lp)
    u = short_conv(u, lp['hy_conv_w'], lp['hy_conv_b'])
    v, x1, x2 = jnp.split(u, 3, axis=-1)
    z = x1 * long_conv(v, kf[:, 0], lp['hy_bias'][0])
    return x2 * long_conv(z, kf[:, 1], lp['hy_bias'][1])

def split_proj(p):
    widths = (Q_COLS, KV_COLS, KV_COLS, SSD_WIDTH, SSD_XBC_COLS, SSD_DT_COLS)
    cuts = []
    total = 0
    for wdt in widths:
        total += wdt
        cuts.append(total)
    return jnp.split(p, cuts, axis=-1)

def merge_groups(att, ssd_y, z, hy, lp):
    ssd_out = rms_norm(ssd_y.reshape(z.shape).astype(z.dtype) * jax.nn.silu(z), lp['ssd_norm'])
    y = jnp.concatenate([rms_norm(att, lp['att_out_norm']), ssd_out,
                         group_rms_norm(hy, lp['hy_out_norm'], HYENA_GROUPS)], axis=-1)
    return y @ lp['w_out']

def hybrid_mixer(hx, hc, rope_cos, rope_sin, lp, ctx_out):
    b, seq_len = hx.shape[:2]
    ctx_len = hc.shape[1]
    q_x, k_x, v_x, z_x, xbc_x, dt_x, hy_x = split_proj(hx @ lp['w_in'])
    q_c, k_c, v_c, z_c, xbc_c, dt_c, hy_c = split_proj(hc @ lp['w_in'])
    scale = HEAD_DIM ** -0.5
    sink = lp['att_sinks'].astype(F32).reshape(ATT_KV_HEADS, ATT_GROUP)
    q_l = apply_axial_rope(rms_norm(_heads(q_x, ATT_HEADS), lp['q_norm']), rope_cos, rope_sin) * scale
    k_l = apply_axial_rope(rms_norm(_heads(k_x, ATT_KV_HEADS), lp['k_norm']), rope_cos, rope_sin)
    k_cx = rms_norm(_heads(k_c, ATT_KV_HEADS), lp['k_norm'])
    v_cx = _heads(v_c, ATT_KV_HEADS)
    att_l = latent_window_attention(q_l.reshape(b, seq_len, ATT_KV_HEADS, ATT_GROUP, HEAD_DIM), k_l,
                                    _heads(v_x, ATT_KV_HEADS), k_cx, v_cx, sink)
    ssd_l, ssd_c = ssd_bidirectional(ssd_prep(xbc_x, dt_x, lp), ssd_prep(xbc_c, dt_c, lp),
                                     lp['ssd_a_log'], lp['ssd_d'], ctx_out)
    y_l = merge_groups(att_l, ssd_l, z_x, hyena_operator(hy_x, lp), lp)
    if not ctx_out:
        return y_l, None
    q_cx = rms_norm(_heads(q_c, ATT_HEADS), lp['q_norm']) * scale
    att_c = context_attention(q_cx.reshape(b, ctx_len, ATT_KV_HEADS, ATT_GROUP, HEAD_DIM), k_cx, v_cx, sink)
    y_c = merge_groups(att_c, ssd_c, z_c, hyena_operator(hy_c, lp), lp)
    return y_l, y_c

def setup_inputs(seed: int = 0) -> dict:
    key = jax.random.key(seed)
    ks = iter(jax.random.split(key, 48))

    def nrm(shape, scale):
        return jax.random.normal(next(ks), shape, F32) * scale

    def gain(shape):
        return 1.0 + 0.05 * jax.random.normal(next(ks), shape, F32)

    n_dense = (DEPTH + 1) // 2
    n_moe = DEPTH // 2
    dt0 = jnp.exp(jax.random.uniform(next(ks), (DEPTH, 2, SSD_HEADS), F32) * (math.log(0.1) - math.log(1e-3)) + math.log(1e-3))
    return {
        'x': nrm((BATCH, SEQ, D_MODEL), 1.0),
        'c': nrm((BATCH, D_MODEL), 1.0),
        'ctx': nrm((BATCH, CTX_LEN, D_MODEL), 1.0),
        'c_ctx': nrm((D_MODEL,), 1.0),
        'w_ada': nrm((DEPTH, D_MODEL, 6 * D_MODEL), 0.5 * D_MODEL ** -0.5),
        'b_ada': nrm((DEPTH, 6 * D_MODEL), 0.02),
        'norm1': gain((DEPTH, D_MODEL)),
        'norm2': gain((DEPTH, D_MODEL)),
        'w_in': nrm((DEPTH, D_MODEL, PROJ_WIDTH), D_MODEL ** -0.5),
        'w_out': nrm((DEPTH, MIX_WIDTH, D_MODEL), MIX_WIDTH ** -0.5),
        'q_norm': gain((DEPTH, HEAD_DIM)),
        'k_norm': gain((DEPTH, HEAD_DIM)),
        'att_sinks': nrm((DEPTH, ATT_HEADS), 0.5),
        'att_out_norm': gain((DEPTH, ATT_WIDTH)),
        'ssd_conv_w': nrm((DEPTH, SSD_CONV, SSD_XBC_COLS), SSD_CONV ** -0.5),
        'ssd_conv_b': nrm((DEPTH, SSD_XBC_COLS), 0.02),
        'ssd_dt_bias': dt0 + jnp.log(-jnp.expm1(-dt0)),
        'ssd_a_log': jnp.log(jax.random.uniform(next(ks), (DEPTH, 2, SSD_HEADS), F32, 1.0, 16.0)),
        'ssd_d': gain((DEPTH, SSD_HEADS)),
        'ssd_norm': gain((DEPTH, SSD_WIDTH)),
        'hy_conv_w': nrm((DEPTH, HYENA_CONV, HY_COLS), HYENA_CONV ** -0.5),
        'hy_conv_b': nrm((DEPTH, HY_COLS), 0.02),
        'hy_w1': nrm((DEPTH, HYENA_POS_DIM, HYENA_FILTER_HIDDEN), HYENA_POS_DIM ** -0.5),
        'hy_b1': nrm((DEPTH, HYENA_FILTER_HIDDEN), 0.1),
        'hy_f1': gain((DEPTH, HYENA_FILTER_HIDDEN)),
        'hy_w2': nrm((DEPTH, HYENA_FILTER_HIDDEN, HYENA_FILTER_HIDDEN), HYENA_FILTER_HIDDEN ** -0.5),
        'hy_b2': nrm((DEPTH, HYENA_FILTER_HIDDEN), 0.1),
        'hy_f2': gain((DEPTH, HYENA_FILTER_HIDDEN)),
        'hy_w3': nrm((DEPTH, HYENA_FILTER_HIDDEN, 2 * HYENA_ORDER * HYENA_WIDTH), 0.02),
        'hy_bias': nrm((DEPTH, HYENA_ORDER, HYENA_WIDTH), 0.1),
        'hy_out_norm': gain((DEPTH, HYENA_WIDTH)),
        'ffn_w_gate': nrm((n_dense, D_MODEL, FFN_DIM), D_MODEL ** -0.5),
        'ffn_w_up': nrm((n_dense, D_MODEL, FFN_DIM), D_MODEL ** -0.5),
        'ffn_w_down': nrm((n_dense, FFN_DIM, D_MODEL), FFN_DIM ** -0.5),
        'moe_router': nrm((n_moe, D_MODEL, N_EXPERTS), D_MODEL ** -0.5),
        'moe_w_gate': nrm((n_moe, N_EXPERTS, D_MODEL, EXPERT_DIM), D_MODEL ** -0.5),
        'moe_w_up': nrm((n_moe, N_EXPERTS, D_MODEL, EXPERT_DIM), D_MODEL ** -0.5),
        'moe_w_down': nrm((n_moe, N_EXPERTS, EXPERT_DIM, D_MODEL), EXPERT_DIM ** -0.5),
    }

def reference(x, c, ctx, c_ctx, w_ada, b_ada, norm1, norm2, w_in, w_out, q_norm, k_norm, att_sinks,
              att_out_norm, ssd_conv_w, ssd_conv_b, ssd_dt_bias, ssd_a_log, ssd_d, ssd_norm, hy_conv_w,
              hy_conv_b, hy_w1, hy_b1, hy_f1, hy_w2, hy_b2, hy_f2, hy_w3, hy_bias, hy_out_norm, ffn_w_gate,
              ffn_w_up, ffn_w_down, moe_router, moe_w_gate, moe_w_up, moe_w_down):
    seq_len = x.shape[1]
    rope_cos, rope_sin = axial_rope_tables(seq_len)
    silu_c = jax.nn.silu(c)
    silu_cc = jax.nn.silu(c_ctx)
    xc = ctx
    for i in range(DEPTH):
        last = i == DEPTH - 1
        lp = {
            'w_in': w_in[i], 'w_out': w_out[i], 'q_norm': q_norm[i], 'k_norm': k_norm[i],
            'att_sinks': att_sinks[i], 'att_out_norm': att_out_norm[i],
            'ssd_conv_w': ssd_conv_w[i], 'ssd_conv_b': ssd_conv_b[i], 'ssd_dt_bias': ssd_dt_bias[i],
            'ssd_a_log': ssd_a_log[i], 'ssd_d': ssd_d[i], 'ssd_norm': ssd_norm[i],
            'hy_conv_w': hy_conv_w[i], 'hy_conv_b': hy_conv_b[i], 'hy_w1': hy_w1[i], 'hy_b1': hy_b1[i],
            'hy_f1': hy_f1[i], 'hy_w2': hy_w2[i], 'hy_b2': hy_b2[i], 'hy_f2': hy_f2[i], 'hy_w3': hy_w3[i],
            'hy_bias': hy_bias[i], 'hy_out_norm': hy_out_norm[i],
        }
        mod = (silu_c @ w_ada[i] + b_ada[i]).reshape(c.shape[0], 6, 1, D_MODEL)
        modc = (silu_cc @ w_ada[i] + b_ada[i]).reshape(6, D_MODEL)
        hx = rms_norm(x, norm1[i]) * (1 + mod[:, 1]) + mod[:, 0]
        hc = rms_norm(xc, norm1[i]) * (1 + modc[1]) + modc[0]
        mix_x, mix_c = hybrid_mixer(hx, hc, rope_cos, rope_sin, lp, not last)
        x = x + mod[:, 2] * mix_x
        x = x + mod[:, 5] * channel_mixer(rms_norm(x, norm2[i]) * (1 + mod[:, 4]) + mod[:, 3], i,
                                          ffn_w_gate, ffn_w_up, ffn_w_down, moe_router, moe_w_gate, moe_w_up, moe_w_down)
        if not last:
            xc = xc + modc[2] * mix_c
            xc = xc + modc[5] * channel_mixer(rms_norm(xc, norm2[i]) * (1 + modc[4]) + modc[3], i,
                                              ffn_w_gate, ffn_w_up, ffn_w_down, moe_router, moe_w_gate, moe_w_up, moe_w_down)
    return x


_drawn_inputs = setup_inputs


def setup_inputs(seed=0):
    import zlib

    import numpy as np

    out = dict(_drawn_inputs(seed))
    spreads = {}
    factors = {'q_norm': 6.307,
     'k_norm': 3.812,
     'att_sinks': 8.0,
     'att_out_norm': 3.07,
     'ssd_conv_b': 5.798,
     'ssd_d': 4.926,
     'ssd_norm': 3.32,
     'hy_f1': 3.03,
     'hy_f2': 3.249,
     'hy_out_norm': 3.292}
    for name, (base, spread) in spreads.items():
        noise = np.random.default_rng([zlib.crc32(name.encode()), seed]).standard_normal(out[name].shape)
        drawn = base * np.exp(spread * noise) if base else spread * noise
        out[name] = jnp.asarray(drawn.astype(out[name].dtype))
    for name, factor in factors.items():
        out[name] = (out[name] * factor).astype(out[name].dtype)
    return out
```

```python
import math
from contextlib import ExitStack

import concourse.bass as bass
from concourse import mybir

F32 = mybir.dt.float32
ALU = mybir.AluOpType
ACT = mybir.ActivationFunctionType
AX_X = mybir.AxisListType.X

P = 128
D = 1024
KD = D // P
SEQ = 256
NTOK = 2 * SEQ
NB = NTOK // P
DEPTH = 2
HEADS, KV_HEADS, HD = 8, 2, 64
GROUP = HEADS // KV_HEADS
WINDOW = 128
ATT_W = HEADS * HD
SSD_W, SSD_H = 256, 4
HY_W, HY_GROUPS = 256, 4
XBC = 512
COL_Q, COL_K, COL_V, COL_Z = 0, 512, 640, 768
COL_XBC, COL_DT, COL_HY, PROJ = 1024, 1536, 1544, 2312
FFN = 2816
NE = 8
EPS = 1e-6
FSTEP = 256
STEPS = FFN // FSTEP
SLOTS = 3
SLOT_USES = [len(range(s, STEPS, SLOTS)) for s in range(SLOTS)]
NEG = -1.0e30

F_N1, F_N2, F_SW, F_SB, F_HW, F_HB, F_LAYER = 0, 8, 16, 28, 32, 50, 56
F_C = DEPTH * F_LAYER
F_COLS = F_C + 16

PARTS = [("q_norm", 64), ("k_norm", 64), ("att_sinks", 8), ("att_out_norm", 512), ("ssd_dt_bias", 8),
         ("ssd_a_log", 8), ("ssd_d", 4), ("ssd_norm", 256), ("hy_bias", 512), ("hy_out_norm", 256)]
PAR, PAR_COLS = {}, 0
for _name, _n in PARTS:
    PAR[_name] = (PAR_COLS, PAR_COLS + _n)
    PAR_COLS += _n

CPARTS = [("ident", P), ("tri_f", P), ("tri_r", P), ("neg_f", P), ("neg_r", P), ("mask", 4 * SEQ),
          ("cos", 2 * 32), ("sin", 2 * 32), ("dft_c", 512), ("dft_s", 512), ("inv_c", 512), ("inv_s", 512),
          ("ones", P), ("iota", P), ("rank8", 8), ("sel", 256)]
FILT_PARTS = [("decay0", 512), ("decay1", 512), ("pos", SEQ)]
CON, CON_COLS = {}, 0
for _name, _n in CPARTS:
    CON[_name] = (CON_COLS, CON_COLS + _n)
    CON_COLS += _n
FILT, FILT_COLS = {}, 0
for _name, _n in FILT_PARTS:
    FILT[_name] = (FILT_COLS, FILT_COLS + _n)
    FILT_COLS += _n


class Counts:

    def __init__(self, eng, own):
        self.eng, self.own, self.told, self.heard, self.last = eng, own, {}, {}, None

    def tell(self, ins, sem):
        ins.then_inc(sem, 1)
        self.told[sem] = self.told.get(sem, 0) + 1
        self.last = (sem, self.told[sem])

    def done(self):
        self.eng.wait_ge(*self.last)

    def link(self, ins):
        self.tell(ins, self.own)
        self.done()

    def hear(self, sem, k=1):
        self.heard[sem] = self.heard.get(sem, 0) + k
        self.eng.wait_ge(sem, self.heard[sem])


class Ring:

    def __init__(self, counts, banks, full, free):
        self.c, self.banks, self.full, self.free, self.n = counts, banks, full, free, 0

    def bank(self):
        return self.banks[self.n % len(self.banks)]

    def open(self):
        b = self.bank()
        if self.n >= len(self.banks):
            self.c.eng.wait_ge(self.free, self.n - len(self.banks) + 1)
        self.n += 1
        return b

    def close(self, ins):
        ins.then_inc(self.full, 1)

    def drained(self):
        self.c.eng.wait_ge(self.free, self.n)

    def take(self):
        b = self.bank()
        self.n += 1
        self.c.eng.wait_ge(self.full, self.n)
        return b

    def give(self, ins):
        self.c.tell(ins, self.free)


def hybrid_block(nc, A, out):
    with ExitStack() as ctx:
        def sb(name, cols):
            return ctx.enter_context(nc.sbuf_tensor(name, [P, cols], F32))

        def sem(name):
            return ctx.enter_context(nc.semaphore(name))

        bank = [ctx.enter_context(nc.psum_tensor(f"bank{i}", [P, 512], F32)) for i in range(8)]
        V_BANKS, A_BANKS, O_BANKS = bank[0:3], bank[3:6], bank[6:8]

        ring = sb("ring", SLOTS * 6144)
        const = sb("const", CON_COLS)
        feat = sb("feat", F_COLS)
        params = sb("params", PAR_COLS)
        X = sb("X", NB * D)
        GATE = sb("GATE", 4 * D)
        HTY = sb("HTY", KD * NTOK + NB * D)
        HT, Y = HTY[:, 0:KD * NTOK], HTY[:, KD * NTOK:KD * NTOK + NB * D]
        HYE = sb("HYE", 3072)
        XBCS = sb("XBCS", 2048)
        WORK = sb("WORK", 5632)
        small = sb("small", 1024)

        x_v = X[:, :].rearrange("p (b d) -> p b d", b=NB)
        ht = HT.rearrange("p (k t) -> p k t", k=KD)
        gate = GATE[:, :].rearrange("p (g s d) -> p g s d", g=2, s=2)
        y_v = Y.rearrange("p (b d) -> p b d", b=NB)
        wslot = [ring[:, i * 4096:(i + 1) * 4096] for i in range(2)]
        tokp = ring[:, 8192:12288].rearrange("p (b d) -> p b d", b=NB)
        xbcp = ring[:, 12288:14352].rearrange("p (c s t) -> p c s t", c=4, s=2)
        hyp = ring[:, 14352:17448].rearrange("p (c s t) -> p c s t", c=6, s=2)
        rows = HTY[0:2, 0:6 * D]
        hyu = WORK[:, 0:3072].rearrange("p (b d) -> p b d", b=NB)
        spec = HYE[:, 0:2048].rearrange("p (r m d) -> p r m d", r=2, m=2)
        conv = HYE[:, 2048:3072].rearrange("p (i d) -> p i d", i=2)
        xbcs = XBCS[:, :].rearrange("p (c t) -> p c t", c=4)
        xsb = ring[:, 12288:12288 + 4 * 384].rearrange("p (b d) -> p b d", b=NB)
        qt = WORK[:, 0:2048].rearrange("p (j t) -> p j t", j=4)
        kt = WORK[:, 2048:2560]
        sc = WORK[:, 2560:3584].rearrange("p (i d) -> p i d", i=2)
        pr = WORK[:, 3584:4608].rearrange("p (i d) -> p i d", i=2)
        pt = WORK[:, 4608:5632].rearrange("p (i d) -> p i d", i=2)
        qn = WORK[:, 2560:3200]
        rope_a = WORK[:, 3200:3520]
        rope_b = WORK[:, 3520:3840]
        qr = WORK[:, 3840:5120].rearrange("p (i d) -> p i d", i=2)
        xn = WORK[:, 0:4096].rearrange("p (b d) -> p b d", b=NB)
        junk = WORK[:, 4096:5120]
        hin = WORK[:, 0:2048].rearrange("p (r b d) -> p r b d", r=2, b=NB)
        decay = WORK[:, 2048:3072].rearrange("p (r h l) -> p r h l", r=2, h=4)
        mix = WORK[:, 3072:3584].rearrange("p (h l) -> p h l", h=4)
        xw = WORK[:, 3584:4096].rearrange("p (r d) -> p r d", r=2)
        ssdt = WORK[:, 4096:5120].rearrange("p (i d) -> p i d", i=4)
        ssdy = WORK[:, 5120:5632].rearrange("p (i d) -> p i d", i=2)
        ur = HT[:, 0:1024].rearrange("p (m d) -> p m d", m=2)
        ui = HT[:, 1024:2048].rearrange("p (m d) -> p m d", m=2)
        yr = HT[:, 2048:3072].rearrange("p (m d) -> p m d", m=2)
        yi = HT[:, 3072:4096].rearrange("p (m d) -> p m d", m=2)
        fw1 = WORK[0:33, 0:64]
        fw2 = WORK[0:64, 64:128]
        fw3 = WORK[0:64, 128:1152]
        fbf = WORK[0:64, 1152:1156]
        farg = WORK[0:64, 1280:1536]
        fk = WORK[0:64, 1536:1792]
        fh = [WORK[0:64, 1792:2048], WORK[0:64, 2048:2304]]
        fp = XBCS[:, 0:1024].rearrange("p (t d) -> p t d", t=2)
        fq = XBCS[:, 1024:2048].rearrange("p (t d) -> p t d", t=2)
        fd = [ring[:, 8192:8704], ring[:, 8704:9216]]
        h2 = WORK[:, 0:2048].rearrange("p (b d) -> p b d", b=2)
        xe = WORK[:, 2048:3072].rearrange("p (k r) -> p k r", k=KD)
        gm = WORK[:, 3072:3328].rearrange("p (b r) -> p b r", b=2)
        gt = WORK[:, 3328:3584]
        ye = WORK[:, 3584:4608]
        sg = [XBCS[:, 256 * b:256 * b + 256] for b in range(2)]
        av = [XBCS[:, 512 + 256 * b:768 + 256 * b] for b in range(2)]
        at = [XBCS[:, 1024 + 256 * b:1280 + 256 * b].rearrange("p (f t) -> p f t", f=2) for b in range(2)]

        used = [0]

        def sm(n):
            used[0] += n
            assert used[0] <= 1024
            return small[:, used[0] - n:used[0]]

        silu_c = sm(16).rearrange("p (k s) -> p k s", s=2)
        coef = sm(64).rearrange("p (w k s) -> p w k s", w=4, s=2)
        ssum, srst = sm(8), sm(8)
        qsum, qrst = sm(40).rearrange("p (b h) -> p b h", b=NB), sm(40).rearrange("p (b h) -> p b h", b=NB)
        rawm, negm, psumr = [sm(16).rearrange("p (i h) -> p i h", i=2) for _ in range(3)]
        qgain = sm(64)
        mhalf = sm(64)
        rden = sm(8)
        snk = sm(8)
        dtu = sm(32).rearrange("p (b h) -> p b h", b=NB)
        dte = sm(32).rearrange("p (b h) -> p b h", b=NB)
        dt = sm(32).rearrange("p (b h) -> p b h", b=NB)
        dta = sm(32).rearrange("p (b h) -> p b h", b=NB)
        aexp = sm(8)
        la = sm(64).rearrange("p (b h) -> p b h", b=NB)
        wend = sm(32).rearrange("p (b h) -> p b h", b=NB)
        ela = sm(64).rearrange("p (b h) -> p b h", b=NB)
        gs, grst = sm(16).rearrange("p (b h) -> p b h", b=NB), sm(16).rearrange("p (b h) -> p b h", b=NB)
        logit = sm(16).rearrange("p (b e) -> p b e", b=2)
        eq = sm(16).rearrange("p (b e) -> p b e", b=2)
        top = sm(8).rearrange("p (w b) -> p w b", w=4)
        hot = sm(32).rearrange("p (w b e) -> p w b e", w=2, b=2)
        sel = sm(16).rearrange("p (b e) -> p b e", b=2)
        pos = sm(16).rearrange("p (b e) -> p b e", b=2)
        over, before = sm(8), sm(8)
        pe_col = sm(2)
        comb = sm(16).rearrange("p (b e) -> p b e", b=2)
        ce = sm(2)
        router = sm(KD * NE).rearrange("p (k e) -> p k e", k=KD)

        fconst = HTY[:, 6 * D:6 * D + FILT_COLS]

        def fcon(name):
            return fconst[:, FILT[name][0]:FILT[name][1]]

        table = ctx.enter_context(nc.sbuf_tensor("table", [P, 2 * NE + 1], mybir.dt.int32))

        def con(name):
            return const[:, CON[name][0]:CON[name][1]]

        def par(name):
            return params[:, PAR[name][0]:PAR[name][1]]

        ident = con("ident")
        dft = {n: con(n).rearrange("p (t f) -> p t f", t=2) for n in ("dft_c", "dft_s", "inv_c", "inv_s")}

        const_in, feat_in, x_in, par_in, b_in = sem("const_in"), sem("feat_in"), sem("x_in"), sem("par_in"), sem("b_in")
        filt_in, router_in, out_done = sem("filt_in"), sem("router_in"), sem("out_done")
        tile_in = [sem("tile_loaded0"), sem("tile_loaded1")]
        slot_in = [sem(f"slot_loaded{i}") for i in range(SLOTS)]
        slot_used = sem("slot_used")
        v_full, v_free, a_full, a_free = sem("v_full"), sem("v_free"), sem("a_full"), sem("a_free")
        vec_own, act_own, pool_own = sem("vec_own"), sem("act_own"), sem("pool_own")
        silu_c_ready, modcol_ready, coef_ready = sem("silu_c_ready"), sem("modcol_ready"), sem("coef_ready")
        sq_ready, pow_asked, pow_ready, xn_ready = sem("sq_ready"), sem("pow_asked"), sem("pow_ready"), sem("xn_ready")
        pads_ready, arg_ready, sin_ready, fpq_ready = (
            sem("pads_ready"), sem("arg_ready"), sem("sin_ready"), sem("fpq_ready"))
        qr_ready, sc_ready, p_ready, o_full, o_free = (
            sem("qr_ready"), sem("sc_ready"), sem("p_ready"), sem("o_full"), sem("o_free"))
        act_asked, act_did = sem("act_asked"), sem("act_did")
        conv_ready, xbc_ready, zs_ready, dta_ready = (
            sem("conv_ready"), sem("xbc_ready"), sem("zs_ready"), sem("dta_ready"))
        dec_ready, xw_ready, h_ready = sem("dec_ready"), sem("xw_ready"), sem("h_ready")
        hconv_ready, hz_ready, yspec_ready = sem("hconv_ready"), sem("hz_ready"), sem("yspec_ready")
        y_ready, x_ready = sem("y_ready"), sem("x_ready")
        gu_full, sg_ready, a_ready, t_full, at_ready, sum_free, ce_ready = (
            sem("gu_full"), sem("sg_ready"), sem("a_ready"), sem("t_full"), sem("at_ready"), sem("sum_free"),
            sem("ce_ready"))
        sel_ready, table_ready, col_ready = sem("sel_ready"), sem("table_ready"), sem("col_ready")
        g_ready, xe_full, xe_ready, gt_full, gt_ready, ye_ready, s_full, s_free = (
            sem("g_ready"), sem("xe_full"), sem("xe_ready"), sem("gt_full"), sem("gt_ready"), sem("ye_ready"),
            sem("s_full"), sem("s_free"))
        layer_done = sem("layer_done")
        FFN_HALVES = 2 * 2 * STEPS

        IN_TILES = [(0, 512), (512, 1024), (1024, 1536), (1536, 1544 + 384), (1544 + 384, 2312)]
        TILES = 12 + len(IN_TILES) + 2

        def tiles(layer):
            for t in range(12):
                yield A["w_ada"][layer, :, 512 * t:512 * t + 512], 512
            for lo, hi in IN_TILES:
                yield A["w_in"][layer, :, lo:hi], hi - lo
            for t in range(2):
                yield A["w_out"][layer, :, 512 * t:512 * t + 512], 512

        def tile_view(i, n):
            return wslot[i][:, 0:KD * n].rearrange("p (k n) -> p k n", k=KD)

        def slot_views(s):
            base = ring[:, s * 6144:(s + 1) * 6144]
            return (base[:, 0:4096].rearrange("p (k w f) -> p k w f", k=KD, w=2),
                    base[:, 4096:6144].rearrange("p (f d) -> p f d", f=2))

        def second_turn(eng, e):
            again = eng.value_load(table[0:1, bass.ds(e * 2, 1)], min_val=0, max_val=1)
            n = eng.value_load(table[0:1, bass.ds(e * 2 + 1, 1)], min_val=NE, max_val=2 * NE)
            return again, n

        tile_done = []
        marks = {}

        def blocks_out(layer):
            return range(NB) if layer < DEPTH - 1 else range(2)

        def seqs_out(layer):
            return len(blocks_out(layer)) // 2

        def units(layer):
            return [(b, h) for b in blocks_out(layer) for h in range(HEADS)]

        def keys_of(b):
            return (0, NTOK) if b < 2 else (SEQ, NTOK)

        def bc(ap, n):
            return ap.unsqueeze(len(ap.shape)).broadcast_to(list(ap.shape) + [n])

        def bc_in(ap, n):
            return ap.unsqueeze(1).broadcast_to([ap.shape[0], n] + list(ap.shape[1:]))

        FWD_NEXT = {2: 3, 3: 0, 0: 1}
        REV_NEXT = {3: 2, 2: 1, 1: 0}
        NEXT = [FWD_NEXT, REV_NEXT]
        FIRST = [2, 3]

        block = ctx.enter_context(nc.Block())

        @block.tensor
        def _(pe):
            c = Counts(pe, None)
            V = Ring(c, V_BANKS, v_full, v_free)
            S = Ring(c, A_BANKS, a_full, a_free)
            tile_no = [0]

            def mm(o, lhsT, rhs, start=True, stop=True):
                return nc.tensor.matmul(o, lhsT, rhs, start=start, stop=stop)

            def tile(n):
                g = tile_no[0]
                tile_no[0] += 1
                pe.wait_ge(tile_in[g % 2], 16 * (g // 2 + 1))
                return tile_view(g % 2, n)

            def tile_ends(r):
                tile_done.append((r.full, r.n))

            def over_k(o, lhsT, rhs):
                for k in range(KD):
                    last = mm(o, lhsT(k), rhs(k), start=(k == 0), stop=(k == KD - 1))
                return last

            def filters(layer):
                pe.wait_ge(filt_in, 80 * (layer + 1))
                b = V.open()
                V.close(mm(b[0:64, 0:SEQ], fw1, fcon("pos")[0:33, :]))
                c.hear(sin_ready)
                b = V.open()
                V.close(mm(b[0:64, 0:SEQ], fw2, fh[0]))
                c.hear(sin_ready)
                for t in range(2):
                    for d in range(2):
                        b = V.open()
                        V.close(mm(b[:, :], fh[1][:, t * P:t * P + P], fw3[:, d * 512:d * 512 + 512]))
                c.hear(fpq_ready)
                for n, src in (("dft_c", fp), ("dft_s", fq)):
                    for m in range(2):
                        b = S.open()
                        mm(b[:, :], dft[n][:, 0, m * P:m * P + P], src[:, 0, :], True, False)
                        S.close(mm(b[:, :], dft[n][:, 1, m * P:m * P + P], src[:, 1, :], False, True))

            def modulation(layer):
                if layer == 0:
                    c.hear(silu_c_ready)
                for t in range(12):
                    w = tile(512)
                    b = V.open()
                    V.close(over_k(b[0:2, :], lambda k: silu_c[:, k, :], lambda k: w[:, k, :]))
                    tile_ends(V)
                V.drained()
                b = S.open()
                for i, wh in enumerate((0, 1, 3, 4)):
                    for k in range(KD):
                        at_ = (i * KD + k) * 2
                        last = nc.tensor.transpose(b[:, at_:at_ + 2], rows[:, wh * D + k * P:wh * D + k * P + P],
                                                   ident[0:2, 0:2])
                S.close(last)
                marks["modcol", layer] = S.n
                for wh in (2, 5):
                    for s in range(2):
                        for half in range(2):
                            b = S.open()
                            lo = wh * D + half * 512
                            S.close(mm(b[:, :], con("sel")[0:2, s * P:s * P + P], rows[:, lo:lo + 512]))

            def to_features(src, blocks, ready=None):
                for b in blocks:
                    if ready is not None:
                        c.hear(ready)
                    for i, r in enumerate((S, V)):
                        o = r.open()
                        for k in range(4):
                            kk = 4 * i + k
                            last = nc.tensor.transpose(o[:, k * P:k * P + P], src[:, b, kk * P:kk * P + P], ident)
                        r.close(last)

            def projections(layer):
                S.drained()
                V.drained()
                w = tile(512)
                for b in blocks_out(layer):
                    o = V.open()
                    V.close(over_k(o[:, :], lambda k: ht[:, k, b * P:b * P + P], lambda k: w[:, k, :]))
                tile_ends(V)
                w = tile(512)
                for b in range(NB):
                    o = S.open()
                    S.close(over_k(o[:, :], lambda k: ht[:, k, b * P:b * P + P], lambda k: w[:, k, :]))
                tile_ends(S)
                marks["kv", layer] = S.n
                w = tile(512)
                for ch in range(4):
                    o = S.open()
                    S.close(over_k(o[:, :], lambda k: w[:, k, ch * P:ch * P + P], lambda k: ht[:, k, :]))
                tile_ends(S)
                marks["xbc", layer] = S.n
                n = SEQ * seqs_out(layer)
                w = tile(8 + 384)
                o = V.open()
                for b in range(NB):
                    last = over_k(o[:, b * 8:b * 8 + 8], lambda k: ht[:, k, b * P:b * P + P], lambda k: w[:, k, 0:8])
                V.close(last)
                for ch in range(3):
                    o = V.open()
                    V.close(over_k(o[:, 0:n], lambda k: w[:, k, 8 + ch * P:8 + ch * P + P], lambda k: ht[:, k, 0:n]))
                tile_ends(V)
                w = tile(384)
                for ch in range(3):
                    o = S.open()
                    S.close(over_k(o[:, 0:n], lambda k: w[:, k, ch * P:ch * P + P], lambda k: ht[:, k, 0:n]))
                tile_ends(S)
                marks["hy", layer] = S.n

            def attention(layer):
                for b in range(NB):
                    c.hear(qr_ready)
                    q = qr[:, b % 2, :]
                    if b in blocks_out(layer):
                        o = S.open()
                        for j in range(4):
                            last = nc.tensor.transpose(o[:, j * P:j * P + P], q[:, j * P:j * P + P], ident)
                        S.close(last)
                    o = V.open()
                    V.close(nc.tensor.transpose(o[:, 0:P], q[:, 512:640], ident))
                    marks["turned", layer, b] = V.n
                S.drained()
                V.drained()
                us = units(layer)
                turned = {}
                for i in range(len(us) + 2):
                    if i < len(us):
                        b, h = us[i]
                        g, j = h // GROUP, h % GROUP
                        lo, hi = keys_of(b)
                        o = V.open()
                        V.close(mm(o[:, 0:hi - lo], qt[64 * g:64 * g + 64, j, b * P:b * P + P],
                                   kt[64 * g:64 * g + 64, lo:hi]))
                    if 1 <= i <= len(us):
                        b, h = us[i - 1]
                        lo, hi = keys_of(b)
                        c.hear(p_ready)
                        o = S.open()
                        for x in range((hi - lo) // P):
                            last = nc.tensor.transpose(o[:, x * P:x * P + P], pr[:, (i - 1) % 2, x * P:x * P + P],
                                                       ident)
                        S.close(last)
                        turned[i - 1] = S.n
                    if i >= 2:
                        b, h = us[i - 2]
                        lo, hi = keys_of(b)
                        g, n = h // GROUP, (hi - lo) // P
                        pe.wait_ge(a_free, turned[i - 2])
                        if h == 0 and b >= 2:
                            c.hear(o_free)
                        for x in range(n):
                            kb = lo // P + x
                            last = mm(O_BANKS[b % 2][:, h * HD:h * HD + HD], pt[:, (i - 2) % 2, x * P:x * P + P],
                                      tokp[:, kb, COL_V + g * HD:COL_V + g * HD + HD], x == 0, x == n - 1)
                        if h == HEADS - 1:
                            last.then_inc(o_full, 1)

            def ssd(layer):
                c.hear(xbc_ready, 4)
                for b in range(NB):
                    o = S.open()
                    for ch in range(3):
                        last = nc.tensor.transpose(o[:, ch * P:ch * P + P], xbcs[:, ch, b * P:b * P + P], ident)
                    S.close(last)
                marks["xsb", layer] = S.n
                c.hear(dta_ready)
                o = V.open()
                for b in range(NB):
                    mm(o[:, b * 16:b * 16 + 4], con("tri_f"), dta[:, b, 0:4])
                    mm(o[:, b * 16 + 4:b * 16 + 8], con("tri_r"), dta[:, b, 4:8])
                    last = mm(o[:, b * 16 + 8:b * 16 + 16], con("ones"), dta[:, b, :])
                V.close(last)
                for b in range(NB):
                    c.hear(xw_ready)
                    o = V.open()
                    V.close(mm(o[:, :], xsb[:, b, 256:384], xw[:, :, :]))
                c.hear(h_ready)
                for b in blocks_out(layer):
                    for r, tri in enumerate(("tri_f", "tri_r")):
                        o = V.open()
                        for h in range(SSD_H):
                            last = mm(o[:, h * P:h * P + P],
                                      dta[:, b, r * 4 + h:r * 4 + h + 1].broadcast_to([P, P]), con(tri))
                        V.close(last)
                        marks["seg", layer, b, r] = V.n
                    for g in range(2):
                        o = V.open()
                        V.close(mm(o[:, 0:P], xbcs[64 * g:64 * g + 64, 2, b * P:b * P + P],
                                   xbcs[64 * g:64 * g + 64, 3, b * P:b * P + P]))
                    mixed = V.n
                    rs = [r for r in range(2) if FIRST[r] != b]
                    for g in range(2):
                        o = V.open()
                        for r in rs:
                            last = mm(o[:, r * P:r * P + P], xbcs[64 * g:64 * g + 64, 3, b * P:b * P + P],
                                      hin[64 * g:64 * g + 64, r, b, g * P:g * P + P])
                        V.close(last)
                    pe.wait_ge(v_free, mixed)
                    o = V.open()
                    for h in range(SSD_H):
                        last = mm(o[:, h * HD:h * HD + HD], mix[:, h, :], xsb[:, b, h * HD:h * HD + HD])
                    V.close(last)

            def hyena(layer):
                ns = seqs_out(layer)
                nb, n = 2 * ns, SEQ * ns
                hyu_st = hyu.rearrange("p (s t) d -> p s t d", t=2)
                for ch in range(6):
                    c.hear(hconv_ready)
                    o = S.open()
                    for b in range(nb):
                        last = nc.tensor.transpose(o[:, b * P:b * P + P], conv[:, ch % 2, b * P:b * P + P], ident)
                    S.close(last)
                    marks["hturned", layer, ch] = S.n
                S.drained()
                for order in range(2):
                    if order == 1:
                        c.hear(hz_ready, 2)
                    for m in range(2):
                        for name in ("dft_c", "dft_s"):
                            o = S.open()
                            for t in range(2):
                                last = mm(o[:, 0:n], dft[name][:, t, m * P:m * P + P], hyu_st[:, 0:ns, t, 0:256],
                                          t == 0, t == 1)
                            S.close(last)
                        marks["dft", layer, order, m] = S.n
                    c.hear(yspec_ready, 2)
                    for t in range(2):
                        o = V.open()
                        for m in range(2):
                            mm(o[:, 0:n], dft["inv_c"][:, m, t * P:t * P + P], yr[:, m, 0:n], m == 0, False)
                            last = mm(o[:, 0:n], dft["inv_s"][:, m, t * P:t * P + P], yi[:, m, 0:n], False, m == 1)
                        V.close(last)

            def output(layer):
                c.hear(y_ready)
                to_features(y_v, blocks_out(layer))
                S.drained()
                V.drained()
                for half in range(2):
                    w = tile(512)
                    for b in blocks_out(layer):
                        o = V.open()
                        V.close(over_k(o[:, :], lambda k: ht[:, k, b * P:b * P + P], lambda k: w[:, k, :]))
                    tile_ends(V)

            def route():
                pe.wait_ge(router_in, 16)
                o = V.open()
                for b in range(2):
                    last = over_k(o[:, b * NE:b * NE + NE], lambda k: ht[:, k, b * P:b * P + P],
                                  lambda k: router[:, k, :])
                V.close(last)
                for b in range(2):
                    for half in range(2):
                        o = S.open()
                        for k in range(4):
                            last = nc.tensor.transpose(o[:, k * P:k * P + P],
                                                       ht[:, 4 * half + k, b * P:b * P + P], ident)
                        S.close(last)
                c.hear(sel_ready)
                o = V.open()
                mm(o[:, 0:8], con("tri_f"), sel[:, 0, :])
                mm(o[:, 8:16], con("tri_f"), sel[:, 1, :], True, False)
                mm(o[:, 8:16], con("ones"), sel[:, 0, :], False, True)
                mm(o[:, 16:24], con("ones"), sel[:, 0, :], True, False)
                V.close(mm(o[:, 16:24], con("ones"), sel[:, 1, :], False, True))
                V.drained()
                S.drained()

            def gather(j):
                pe.wait_ge(g_ready, j + 1)
                for i in range(2):
                    for k in range(4):
                        for b in range(2):
                            last = mm(bank[5 + i][:, k * P:k * P + P],
                                      h2[:, b, (4 * i + k) * P:(4 * i + k) * P + P], gm[:, b, :], b == 0, b == 1)
                    last.then_inc(xe_full, 1)

            def turn_gather(j):
                for b in range(2):
                    last = nc.tensor.transpose(bank[7][:, b * P:b * P + P], gm[:, b, :], ident)
                last.then_inc(gt_full, 1)

            def expert_job(j, has_next):
                def hidden(s, k0, k1):
                    gu, _ = slot_views(s % SLOTS)
                    for k in range(k0, k1):
                        last = mm(bank[2 + s % 2][:, :], xe[:, k, :], gu[:, k, :, :], k == 0, k == KD - 1)
                    if k1 == KD:
                        last.then_inc(gu_full, 1)

                def turn(s):
                    pe.wait_ge(a_ready, j * STEPS + (FFN_HALVES + s + 1))
                    for f in range(2):
                        last = nc.tensor.transpose(bank[4][:, f * P:f * P + P], av[0][:, f * P:f * P + P], ident)
                    last.then_inc(t_full, 1)

                def down(s):
                    _, dn = slot_views(s % SLOTS)
                    pe.wait_ge(at_ready, j * STEPS + (FFN_HALVES + s + 1))
                    for f in range(2):
                        for half in range(2):
                            last = mm(bank[half][:, :], at[0][:, f, :], dn[:, f, half * 512:half * 512 + 512],
                                      s == 0 and f == 0, s == STEPS - 1 and f == 1)
                    last.then_inc(slot_used, 1)

                pe.wait_ge(xe_ready, j * 2 + 2)
                for s in range(STEPS):
                    i = s % SLOTS
                    pe.wait_ge(slot_in[i], j * (SLOT_USES[i] * 48) + (2 * SLOT_USES[i] + s // SLOTS + 1) * 48)
                    hidden(s, 0, 4)
                    if s:
                        turn(s - 1)
                    hidden(s, 4, KD)
                    if s:
                        down(s - 1)
                if has_next:
                    gather(j + 1)
                turn(STEPS - 1)
                down(STEPS - 1)
                pe.wait_ge(ye_ready, j * 2 + 2)
                pe.wait_ge(gt_ready, j + 1)
                for i in range(4):
                    if i == 3:
                        pe.wait_ge(s_free, j * 4 + 2)
                    t, half = i // 2, i % 2
                    mm(bank[5 + i % 3][:, :], gt[:, t * P:t * P + P], ye[:, half * 512:half * 512 + 512]
                       ).then_inc(s_full, 1)
                pe.wait_ge(s_free, j * 4 + 5)
                if has_next:
                    turn_gather(j + 1)

            def ffn_job(J, b0, first):
                def hidden(b, k0, k1):
                    for k in range(k0, k1):
                        last = mm(bank[4 + b][:, :], ht[:, k, (b0 + b) * P:(b0 + b) * P + P],
                                  gu[:, k, :, :], k == 0, k == KD - 1)
                    if k1 == KD:
                        last.then_inc(gu_full, 1)

                def turn(b):
                    pe.wait_ge(a_ready, n + b + 1)
                    for f in range(2):
                        last = nc.tensor.transpose(bank[6 + b][:, f * P:f * P + P], av[b][:, f * P:f * P + P], ident)
                    last.then_inc(t_full, 1)

                def down(b, parts):
                    for f, half in parts:
                        last = mm(bank[2 * b + half][:, :], at[b][:, f, :], dn[:, f, half * 512:half * 512 + 512],
                                  s == 0 and f == 0, s == STEPS - 1 and f == 1)
                    return last

                for s in range(STEPS):
                    gu, dn = slot_views(s % SLOTS)
                    n = (J * STEPS + s) * 2
                    pe.wait_ge(slot_in[s % SLOTS], (J * SLOT_USES[s % SLOTS] + s // SLOTS + 1) * 48)
                    hidden(0, 0, KD)
                    hidden(1, 0, 4)
                    turn(0)
                    hidden(1, 4, KD)
                    if s == 0 and not first:
                        pe.wait_ge(sum_free, J)
                    pe.wait_ge(at_ready, n + 1)
                    down(0, [(0, 0), (0, 1), (1, 0)])
                    turn(1)
                    down(0, [(1, 1)])
                    pe.wait_ge(at_ready, n + 2)
                    down(1, [(0, 0), (0, 1), (1, 0), (1, 1)]).then_inc(slot_used, 1)

            pe.wait_ge(const_in, 16)
            for layer in range(DEPTH):
                filters(layer)
                modulation(layer)
                to_features(xn, range(NB), xn_ready)
                projections(layer)
                attention(layer)
                ssd(layer)
                hyena(layer)
                output(layer)
                to_features(xn, blocks_out(layer), xn_ready)
                S.drained()
                V.drained()
                if layer == 0:
                    c.hear(o_free, 2)
                    ffn_job(0, 0, True)
                    ffn_job(1, 2, False)
                else:
                    route()
                    c.hear(o_free, 2)
                    gather(0)
                    turn_gather(0)
                    with pe.Fori(0, NE - 1) as e:
                        expert_job(e, True)
                    expert_job(NE - 1, False)
                    pe.wait_ge(table_ready, 1)
                    with pe.Fori(0, NE) as e:
                        again, n = second_turn(pe, e)
                        with pe.If(again):
                            gather(n)
                            turn_gather(n)
                            expert_job(n, False)

        @block.sync
        def _(sp):
            c = Counts(sp, None)
            sp.sem_inc(slot_used, SLOTS)
            sp.dma_start(const[:, :], A["const"]).then_inc(const_in, 16)
            sp.dma_start(feat[:, :], A["feat"]).then_inc(feat_in, 16)
            sp.dma_start(x_v[:, 0:2, :], A["x"][0].rearrange("(b p) d -> p b d", p=P)).then_inc(x_in, 16)
            sp.dma_start(x_v[:, 2:4, :], A["ctx"][0].rearrange("(b p) d -> p b d", p=P)).then_inc(x_in, 16)

            def ffn_loads(J, wg, wu, wd):
                for s in range(STEPS):
                    gu, dn = slot_views(s % SLOTS)
                    i = s % SLOTS
                    before = s - SLOTS if s >= SLOTS else i + SLOTS * (SLOT_USES[i] - 1) - STEPS
                    sp.wait_ge(slot_used, J * STEPS + (before + 1 + SLOTS))
                    lo, hi = s * FSTEP, (s + 1) * FSTEP
                    sp.dma_start(gu[:, :, 0, :], wg[:, lo:hi].rearrange("(k p) f -> p k f", p=P)
                                 ).then_inc(slot_in[i], 16)
                    sp.dma_start(gu[:, :, 1, :], wu[:, lo:hi].rearrange("(k p) f -> p k f", p=P)
                                 ).then_inc(slot_in[i], 16)
                    sp.dma_start(dn, wd[lo:hi, :].rearrange("(f p) d -> p f d", p=P)).then_inc(slot_in[i], 16)

            for layer in range(DEPTH):
                if layer > 0:
                    c.hear(layer_done)
                sp.dma_start(rows, A["b_ada"][layer, :].partition_broadcast(2)).then_inc(b_in, 16)
                sp.dma_start(params[:, :], A["params"][layer, :].partition_broadcast(P)).then_inc(par_in, 16)
                sp.dma_start(fconst, A["filter_const"]).then_inc(filt_in, 16)
                sp.dma_start(fw1, A["hy_w1"][layer]).then_inc(filt_in, 16)
                sp.dma_start(fw2, A["hy_w2"][layer]).then_inc(filt_in, 16)
                sp.dma_start(fw3, A["hy_w3"][layer]).then_inc(filt_in, 16)
                sp.dma_start(fbf, A["hy_bf"][:, 4 * layer:4 * layer + 4]).then_inc(filt_in, 16)
                for i, (src, n) in enumerate(tiles(layer)):
                    g = layer * TILES + i
                    if g >= 2:
                        sp.wait_ge(*tile_done[g - 2])
                    sp.dma_start(tile_view(g % 2, n), src.rearrange("(k p) n -> p k n", p=P)
                                 ).then_inc(tile_in[g % 2], 16)
                sp.wait_ge(*tile_done[(layer + 1) * TILES - 1])
                if layer == 0:
                    for J in range(2):
                        ffn_loads(J, A["ffn_w_gate"][0], A["ffn_w_up"][0], A["ffn_w_down"][0])
                else:
                    sp.dma_start(router, A["moe_router"][0].rearrange("(k p) e -> p k e", p=P)
                                 ).then_inc(router_in, 16)
                    def expert_loads(j, e):
                        ffn_loads(j + 2, *[A[w][0][bass.ds(e, 1)].rearrange("a d f -> (a d) f")
                                           for w in ("moe_w_gate", "moe_w_up", "moe_w_down")])
                    with sp.Fori(0, NE) as e:
                        expert_loads(e, e)
                    sp.wait_ge(table_ready, 1)
                    with sp.Fori(0, NE) as e:
                        again, n = second_turn(sp, e)
                        with sp.If(again):
                            expert_loads(n, e)
            c.hear(layer_done)
            sp.dma_start(out[0].rearrange("(b p) d -> p b d", p=P), x_v[:, 0:2, :]).then_inc(out_done, 16)
            sp.wait_ge(out_done, 16)

        @block.gpsimd
        def _(pool):
            c = Counts(pool, pool_own)
            c.link(nc.gpsimd.memset(mhalf, -0.5))

            def rsqrt(o, i, w):
                c.hear(pow_asked)
                c.tell(nc.gpsimd.tensor_tensor(o, i, w, ALU.pow), pow_ready)

            for layer in range(DEPTH):
                nb = len(blocks_out(layer))
                if layer > 0:
                    c.hear(layer_done)
                nc.gpsimd.memset(xbcp[:, :, :, 0:1], 0.0)
                nc.gpsimd.memset(xbcp[:, :, :, SEQ + 1:SEQ + 2], 0.0)
                nc.gpsimd.memset(hyp[:, :, :, 0:1], 0.0)
                c.tell(nc.gpsimd.memset(hyp[:, :, :, SEQ + 1:SEQ + 2], 0.0), pads_ready)
                h40 = mhalf[:, 0:40].rearrange("p (b h) -> p b h", b=NB)
                rsqrt(srst[:, 0:NB], ssum[:, 0:NB], mhalf[:, 0:NB])
                rsqrt(qrst[:, 0:nb, :], qsum[:, 0:nb, :], h40[:, 0:nb, :])
                if nb < NB:
                    rsqrt(qrst[:, nb:NB, 8:10], qsum[:, nb:NB, 8:10], h40[:, nb:NB, 8:10])
                rsqrt(srst[:, 0:nb], ssum[:, 0:nb], mhalf[:, 0:nb])
                rsqrt(srst[:, 0:nb], ssum[:, 0:nb], mhalf[:, 0:nb])
                h16 = mhalf[:, 0:16].rearrange("p (b h) -> p b h", b=NB)
                rsqrt(grst[:, 0:nb, :], gs[:, 0:nb, :], h16[:, 0:nb, :])
                rsqrt(srst[:, 0:nb], ssum[:, 0:nb], mhalf[:, 0:nb])

        @block.scalar
        def _(act):
            c = Counts(act, act_own)
            S = Ring(c, A_BANKS, a_full, a_free)

            def f(o, i, func, **kw):
                return nc.scalar.activation(o, i, func, **kw)

            def take_copy(o, view=lambda b: b[:, :]):
                b = S.take()
                S.give(f(o, view(b), ACT.Copy))

            def norm(layer, blocks, wh, first):
                if not first:
                    c.hear(x_ready)
                elif layer == 0:
                    act.wait_ge(x_in, 32)
                else:
                    c.hear(layer_done)
                for b in blocks:
                    c.tell(f(junk, x_v[:, b, :], ACT.Square, accum_out=ssum[:, b:b + 1]), sq_ready)
                    c.done()
                if wh == 0:
                    c.hear(coef_ready)
                for b in blocks:
                    o = S.take()
                    s = b // 2
                    for k in range(4):
                        last = f(ht[:, k, b * P:b * P + P], o[:, k * P:k * P + P], ACT.Identity,
                                 scale=coef[:, wh + 1, k, s:s + 1], bias=coef[:, wh, k, s:s + 1])
                    S.give(last)

            def seqs(b):
                return b[:, :].rearrange("p (s t) -> p s t", s=2)

            def attention(layer):
                for b in blocks_out(layer):
                    take_copy(qt[:, :, b * P:b * P + P], lambda o: o[:, :].rearrange("p (j t) -> p j t", j=4))
                us = units(layer)
                for i in range(len(us) + 1):
                    if i < len(us):
                        b, h = us[i]
                        lo, hi = keys_of(b)
                        c.hear(sc_ready)
                        c.tell(f(pr[:, i % 2, 0:hi - lo], sc[:, i % 2, 0:hi - lo], ACT.Exp,
                                 bias=negm[:, b % 2, h:h + 1], accum_out=psumr[:, b % 2, h:h + 1]), p_ready)
                    if i >= 1:
                        b, h = us[i - 1]
                        lo, hi = keys_of(b)
                        take_copy(pt[:, (i - 1) % 2, 0:hi - lo], lambda o: o[:, 0:hi - lo])
                    for b in blocks_out(layer):
                        if i == min(8 * b + 10, len(us)):
                            c.hear(act_asked)
                            c.tell(f(snk, snk, ACT.Exp), act_did)

            def ssd(layer):
                for ch in range(4):
                    c.hear(conv_ready)
                    c.tell(f(xbcs[:, ch, :], conv[:, ch % 2, :], ACT.Silu), xbc_ready)
                for b in blocks_out(layer):
                    c.tell(f(tokp[:, b, COL_Z:D], tokp[:, b, COL_Z:D], ACT.Silu), zs_ready)
                for b in range(NB):
                    take_copy(xsb[:, b, :], lambda o: o[:, 0:384])
                c.hear(act_asked)
                c.link(f(dte, dte, ACT.Exp))
                f(dte, dte, ACT.Ln, bias=con("ones")[:, 0:1])
                c.tell(f(aexp, par("ssd_a_log"), ACT.Exp), act_did)
                c.hear(act_asked)
                f(wend, wend, ACT.Exp)
                c.tell(f(ela, la, ACT.Exp), act_did)
                for b in blocks_out(layer):
                    for r in range(2):
                        act.wait_ge(v_free, marks["seg", layer, b, r])
                        c.tell(f(decay[:, r, :, :], decay[:, r, :, :], ACT.Exp), dec_ready)

            def hyena(layer):
                ns = seqs_out(layer)
                nb, n = 2 * ns, SEQ * ns
                for ch in range(6):
                    take_copy(hyu[:, 0:nb, ch * P:ch * P + P],
                              lambda o: o[:, 0:nb * P].rearrange("p (b d) -> p b d", b=nb))
                for order in range(2):
                    for m in range(2):
                        take_copy(ur[:, m, 0:n], lambda o: o[:, 0:n])
                        take_copy(ui[:, m, 0:n], lambda o: o[:, 0:n])

            def ffn_job(J):
                for s in range(STEPS):
                    n = (J * STEPS + s) * 2
                    for b in range(2):
                        act.wait_ge(gu_full, n + b + 1)
                        f(sg[b], bank[4 + b][:, 0:FSTEP], ACT.Silu).then_inc(sg_ready, 1)
                        act.wait_ge(t_full, n + b + 1)
                        f(at[b], bank[6 + b][:, 0:2 * P].rearrange("p (f t) -> p f t", f=2), ACT.Copy
                          ).then_inc(at_ready, 1)

            def take_gathered(j):
                for i in range(2):
                    act.wait_ge(xe_full, j * 2 + (i + 1))
                    f(xe[:, 4 * i:4 * i + 4, :], bank[5 + i][:, :].rearrange("p (k r) -> p k r", k=4), ACT.Copy
                      ).then_inc(xe_ready, 1)

            def take_turned(j):
                act.wait_ge(gt_full, j + 1)
                f(gt, bank[7][:, 0:2 * P], ACT.Copy).then_inc(gt_ready, 1)

            def expert_job(j, has_next):
                for s in range(STEPS):
                    act.wait_ge(gu_full, j * STEPS + (FFN_HALVES + s + 1))
                    f(sg[0], bank[2 + s % 2][:, 0:FSTEP], ACT.Silu).then_inc(sg_ready, 1)
                    if s == STEPS - 1 and has_next:
                        take_gathered(j + 1)
                    act.wait_ge(t_full, j * STEPS + (FFN_HALVES + s + 1))
                    f(at[0], bank[4][:, 0:2 * P].rearrange("p (f t) -> p f t", f=2), ACT.Copy
                      ).then_inc(at_ready, 1)
                act.wait_ge(slot_used, j * STEPS + (3 * STEPS + SLOTS))
                f(ye[:, 0:512], bank[0][:, :], ACT.Copy).then_inc(ye_ready, 1)
                if has_next:
                    take_turned(j + 1)

            act.wait_ge(feat_in, 16)
            c.tell(f(silu_c, feat[:, F_C:F_C + 16].rearrange("p (s k) -> p k s", s=2), ACT.Silu), silu_c_ready)
            for layer in range(DEPTH):
                for i in range(2):
                    c.hear(arg_ready)
                    c.tell(f(fh[i], farg, ACT.Sin), sin_ready)
                for r in range(2):
                    for m in range(2):
                        take_copy(spec[:, r, m, :])
                o = S.take()
                S.give(f(coef, o[:, 0:64].rearrange("p (w k s) -> p w k s", w=4, s=2), ACT.Copy))
                for g in range(2):
                    for s in range(2):
                        for half in range(2):
                            take_copy(gate[:, g, s, half * 512:half * 512 + 512])
                norm(layer, range(NB), 0, True)
                for b in range(NB):
                    take_copy(tokp[:, b, 512:1024])
                for ch in range(4):
                    take_copy(xbcp[:, ch, :, 1:SEQ + 1], seqs)
                ns = seqs_out(layer)
                for ch in range(3, 6):
                    take_copy(hyp[:, ch, 0:ns, 1:SEQ + 1], lambda o: seqs(o)[:, 0:ns, :])
                attention(layer)
                ssd(layer)
                hyena(layer)
                for b in blocks_out(layer):
                    take_copy(ht[:, 0:4, b * P:b * P + P], lambda o: o[:, :].rearrange("p (k t) -> p k t", k=4))
                norm(layer, blocks_out(layer), 2, False)
                if layer == DEPTH - 1:
                    for b in range(2):
                        for half in range(2):
                            take_copy(h2[:, b, half * 512:half * 512 + 512])
                    c.hear(act_asked)
                    c.tell(f(top[:, 2, :], top[:, 2, :], ACT.Exp), act_did)
                if layer == 0:
                    for J in range(2):
                        ffn_job(J)
                else:
                    take_gathered(0)
                    take_turned(0)
                    with act.Fori(0, NE - 1) as e:
                        expert_job(e, True)
                    expert_job(NE - 1, False)
                    act.wait_ge(table_ready, 1)
                    with act.Fori(0, NE) as e:
                        again, n = second_turn(act, e)
                        with act.If(again):
                            take_gathered(n)
                            take_turned(n)
                            expert_job(n, False)

        @block.vector
        def _(dve):
            v = nc.vector
            c = Counts(dve, vec_own)
            V = Ring(c, V_BANKS, v_full, v_free)
            link = c.link

            def ask_rsqrt():
                c.hear(pow_ready)

            def mean_sq(o, n):
                c.tell(v.tensor_scalar(o, o, 1.0 / n, EPS, ALU.mult, ALU.add), pow_asked)

            def tt(o, a, b, op):
                return v.tensor_tensor(o, a, b, op)

            def filters(layer):
                dve.wait_ge(filt_in, 80 * (layer + 1))
                for i in range(2):
                    o = V.take()
                    V.give(v.tensor_scalar(farg, o[0:64, 0:SEQ], fbf[:, 2 * i:2 * i + 1],
                                           fbf[:, 2 * i + 1:2 * i + 2], ALU.add, ALU.mult))
                    c.done()
                    link(v.tensor_scalar(fk, farg, INV_2PI, ROUND, ALU.mult, ALU.add))
                    link(v.tensor_scalar(fk, fk, ROUND, None, ALU.subtract))
                    for part in TWO_PI:
                        link(v.scalar_tensor_tensor(out=farg, in0=fk, scalar=-part, in1=farg, op0=ALU.mult,
                                                    op1=ALU.add))
                    c.tell(v.tensor_scalar(farg, farg, PI_F, -PI_F, ALU.min, ALU.max), arg_ready)
                for t in range(2):
                    for d in range(2):
                        o = V.take()
                        dec = fcon(f"decay{d}").rearrange("p (t d) -> p t d", t=2)[:, t, :]
                        V.give(tt(fd[d].rearrange("p (o d) -> p o d", o=2),
                                  o[:, :].rearrange("p (o d) -> p o d", o=2), bc_in(dec, 2), ALU.mult))
                    c.done()
                    link(tt(fp[:, t, :], fd[0], fd[1], ALU.add))
                    ins = tt(fq[:, t, :], fd[0], fd[1], ALU.subtract)
                    if t == 0:
                        link(ins)
                    else:
                        c.tell(ins, fpq_ready)

            def modulation(layer):
                dve.wait_ge(b_in, 16 * (layer + 1))
                for t in range(12):
                    o = V.take()
                    V.give(tt(rows[:, 512 * t:512 * t + 512], o[0:2, :], rows[:, 512 * t:512 * t + 512], ALU.add))
                dve.wait_ge(a_free, marks["modcol", layer])
                for w, norm_col in ((1, F_N1), (3, F_N2)):
                    f0 = layer * F_LAYER + norm_col
                    link(v.tensor_scalar(coef[:, w, :, :], coef[:, w, :, :], 1.0, None, ALU.add))
                    ins = tt(coef[:, w, :, :], coef[:, w, :, :], bc(feat[:, f0:f0 + KD], 2), ALU.mult)
                    if w == 1:
                        link(ins)
                    else:
                        c.tell(ins, coef_ready)
                        c.done()

            def norm(blocks, wh):
                blocks = list(blocks)
                c.hear(sq_ready, len(blocks))
                mean_sq(ssum[:, 0:len(blocks)], D)
                ask_rsqrt()
                for b in blocks:
                    c.tell(v.tensor_scalar(xn[:, b, :], x_v[:, b, :], srst[:, b:b + 1], None, ALU.mult), xn_ready)
                for b in blocks:
                    o = V.take()
                    s = b // 2
                    for k in range(4):
                        last = v.tensor_scalar(ht[:, 4 + k, b * P:b * P + P], o[:, k * P:k * P + P],
                                               coef[:, wh + 1, 4 + k, s:s + 1], coef[:, wh, 4 + k, s:s + 1],
                                               ALU.mult, ALU.add)
                    V.give(last)

            def projections(layer):
                ns = seqs_out(layer)
                for b in blocks_out(layer):
                    o = V.take()
                    V.give(v.tensor_copy(tokp[:, b, 0:512], o[:, :]))
                o = V.take()
                V.give(v.tensor_copy(dtu, o[:, 0:32].rearrange("p (b h) -> p b h", b=NB)))
                for ch in range(3):
                    o = V.take()
                    V.give(v.tensor_copy(hyp[:, ch, 0:ns, 1:SEQ + 1],
                                         o[:, 0:ns * SEQ].rearrange("p (s t) -> p s t", s=ns)))

            def attention(layer):
                dve.wait_ge(a_free, marks["kv", layer])
                dve.wait_ge(par_in, 16 * (layer + 1))
                c.done()
                link(v.tensor_scalar(qgain, par("q_norm"), HD ** -0.5, None, ALU.mult))
                nb = len(blocks_out(layer))

                def heads_of(b):
                    return 0 if b < nb else HEADS
                for b in range(NB):
                    h0 = heads_of(b)
                    src = tokp[:, b, h0 * HD:10 * HD]
                    link(tt(qn[:, h0 * HD:640], src, src, ALU.mult))
                    link(v.tensor_reduce(qsum[:, b, h0:10], qn[:, h0 * HD:640].rearrange("p (h d) -> p h d", d=HD),
                                         AX_X, ALU.add))
                mean_sq(qsum[:, 0:nb, :], HD)
                if nb < NB:
                    mean_sq(qsum[:, nb:NB, 8:10], HD)
                    ask_rsqrt()
                ask_rsqrt()
                for b in range(NB):
                    h0 = heads_of(b)
                    if b >= 2:
                        dve.wait_ge(v_full, marks["turned", layer, b - 2])
                    dst = qn if b < 2 else qr[:, b % 2, :]
                    if h0 == 0:
                        q = tokp[:, b, 0:512].rearrange("p (g j d) -> p g j d", g=2, d=HD)
                        link(tt(dst[:, 0:512].rearrange("p (j g d) -> p g j d", g=2, d=HD), q,
                                bc(qrst[:, b, 0:8].rearrange("p (g j) -> p g j", g=2), HD), ALU.mult))
                        q = dst[:, 0:512].rearrange("p (h d) -> p h d", d=HD)
                        link(tt(q, q, bc_in(qgain, 8), ALU.mult))
                    k = dst[:, 512:640].rearrange("p (h d) -> p h d", d=HD)
                    link(tt(k, tokp[:, b, 512:640].rearrange("p (h d) -> p h d", d=HD),
                            bc(qrst[:, b, 8:10], HD), ALU.mult))
                    ins = tt(k, k, bc_in(par("k_norm"), 2), ALU.mult)
                    if b >= 2:
                        c.tell(ins, qr_ready)
                        continue
                    link(ins)

                    def halves(x):
                        x = x.rearrange("p (h a w f) -> p h a w f", a=2, w=2, f=16)
                        return x[:, :, :, 0, :], x[:, :, :, 1, :]
                    x1, x2 = halves(qn)
                    o1, o2 = halves(qr[:, b % 2, :])
                    cs, sn = [bc_in(con(w)[:, 32 * b:32 * b + 32].rearrange("p (a f) -> p a f", a=2), 10)
                              for w in ("cos", "sin")]
                    ra, rb = [x.rearrange("p (h a f) -> p h a f", a=2, f=16) for x in (rope_a, rope_b)]
                    tt(ra, x1, cs, ALU.mult)
                    link(tt(rb, x2, sn, ALU.mult))
                    link(tt(o1, ra, rb, ALU.subtract))
                    tt(ra, x1, sn, ALU.mult)
                    link(tt(rb, x2, cs, ALU.mult))
                    c.tell(tt(o2, ra, rb, ALU.add), qr_ready)
                for b in range(NB):
                    o = V.take()
                    V.give(v.tensor_copy(kt[:, b * P:b * P + P], o[:, 0:P]))
                c.done()
                us = units(layer)
                for i in range(len(us) + 1):
                    if i < len(us):
                        b, h = us[i]
                        lo, hi = keys_of(b)
                        o = V.take()
                        m0 = 512 * b if b < 2 else SEQ
                        V.give(v.tensor_tensor_reduce(out=sc[:, i % 2, 0:hi - lo], in0=o[:, 0:hi - lo],
                                                      in1=con("mask")[:, m0:m0 + hi - lo], scale=1.0, scalar=-3.0e38,
                                                      op0=ALU.add, op1=ALU.max, accum_out=rawm[:, b % 2, h:h + 1]))
                        c.done()
                        c.tell(v.tensor_scalar(negm[:, b % 2, h:h + 1], rawm[:, b % 2, h:h + 1],
                                               par("att_sinks")[:, h:h + 1], -1.0, ALU.max, ALU.mult), sc_ready)
                    for b in blocks_out(layer):
                        if i == min(8 * b + 10, len(us)):
                            c.done()
                            c.tell(tt(snk, negm[:, b % 2, :], par("att_sinks"), ALU.add), act_asked)
                            c.hear(act_did)
                            link(tt(rden, psumr[:, b % 2, :], snk, ALU.add))
                            link(v.reciprocal(rden, rden))
                            c.hear(o_full)
                            y = y_v[:, b, 0:ATT_W]
                            c.tell(tt(y.rearrange("p (h d) -> p h d", d=HD),
                                      O_BANKS[b % 2][:, :].rearrange("p (h d) -> p h d", d=HD),
                                      bc(rden, HD), ALU.mult), o_free)
                            c.done()
                            link(v.tensor_tensor_reduce(out=conv[:, 0, :], in0=y, in1=y, scale=1.0, scalar=0.0,
                                                        op0=ALU.mult, op1=ALU.add, accum_out=ssum[:, b:b + 1]))
                mean_sq(ssum[:, 0:nb], ATT_W)
                ask_rsqrt()
                for b in range(nb):
                    y = y_v[:, b, 0:ATT_W]
                    link(v.scalar_tensor_tensor(out=y, in0=y, scalar=srst[:, b:b + 1], in1=par("att_out_norm"),
                                                op0=ALU.mult, op1=ALU.mult))

            def convolve(o, x, n, w, bias):
                link(v.tensor_scalar(o, x[:, 0:n, 0:SEQ], w(0), bias, ALU.mult, ALU.add))
                link(v.scalar_tensor_tensor(out=o, in0=x[:, 0:n, 1:SEQ + 1], scalar=w(1), in1=o, op0=ALU.mult,
                                            op1=ALU.add))
                return v.scalar_tensor_tensor(out=o, in0=x[:, 0:n, 2:SEQ + 2], scalar=w(2), in1=o, op0=ALU.mult,
                                              op1=ALU.add)

            def fcol(layer, i):
                j = layer * F_LAYER + i
                return feat[:, j:j + 1]

            def ssd(layer):
                nb = len(blocks_out(layer))
                c.hear(pads_ready)
                dve.wait_ge(a_free, marks["xbc", layer])
                for ch in range(4):
                    if ch >= 2:
                        c.hear(xbc_ready)
                    o = conv[:, ch % 2, :].rearrange("p (s t) -> p s t", s=2)
                    c.tell(convolve(o, xbcp[:, ch, :, :], 2, lambda i: fcol(layer, F_SW + 4 * i + ch),
                                    fcol(layer, F_SB + ch)), conv_ready)
                link(tt(dtu, dtu, bc_in(par("ssd_dt_bias"), NB), ALU.add))
                link(v.tensor_scalar(dte, dtu, -1.0, None, ALU.mult))
                c.tell(tt(dte, dtu, dte, ALU.min), act_asked)
                c.hear(act_did)
                c.hear(xbc_ready, 2)
                link(v.scalar_tensor_tensor(out=dt, in0=dtu, scalar=0.0, in1=dte, op0=ALU.max, op1=ALU.add))
                c.tell(v.scalar_tensor_tensor(out=dta, in0=dt, scalar=-1.0, in1=bc_in(aexp, NB), op0=ALU.mult,
                                              op1=ALU.mult), dta_ready)
                o = V.take()
                V.give(v.tensor_copy(la, o[:, 0:64].rearrange("p (b h) -> p b h", b=NB)))
                c.done()
                c.tell(tt(wend, la[:, :, 8:16], la[:, :, 0:8], ALU.subtract), act_asked)
                c.hear(act_did)
                link(tt(wend, wend, dt, ALU.mult))
                dve.wait_ge(a_free, marks["xsb", layer])
                for b in range(NB):
                    x = xsb[:, b, 0:256].rearrange("p (h d) -> p h d", d=HD)
                    for r in range(2):
                        last = tt(xw[:, r, :].rearrange("p (h d) -> p h d", d=HD), x,
                                  bc(wend[:, b, 4 * r:4 * r + 4], HD), ALU.mult)
                    c.tell(last, xw_ready)
                    o = V.take()
                    to = [(r, NEXT[r][b]) for r in range(2) if b in NEXT[r]]
                    for r, nxt in to:
                        last = v.tensor_copy(hin[:, r, nxt, :], o[:, 256 * r:256 * r + 256])
                    V.give(last)
                c.done()
                for i, (r, b) in enumerate(((0, 3), (0, 0), (1, 2), (1, 1))):
                    nxt = NEXT[r][b]
                    link(tt(ssdt[:, 0, :].rearrange("p (h d) -> p h d", d=HD),
                            hin[:, r, b, :].rearrange("p (h d) -> p h d", d=HD),
                            bc(ela[:, b, 8 + 4 * r:12 + 4 * r], HD), ALU.mult))
                    ins = tt(hin[:, r, nxt, :], hin[:, r, nxt, :], ssdt[:, 0, :], ALU.add)
                    if i < 3:
                        link(ins)
                    else:
                        c.tell(ins, h_ready)
                c.hear(zs_ready, nb)
                for b in blocks_out(layer):
                    for r, neg in enumerate(("neg_f", "neg_r")):
                        o = V.take()
                        for h in range(SSD_H):
                            last = v.scalar_tensor_tensor(out=decay[:, r, h, :], in0=o[:, h * P:h * P + P],
                                                          scalar=la[:, b, 4 * r + h:4 * r + h + 1], in1=con(neg),
                                                          op0=ALU.subtract, op1=ALU.add)
                        V.give(last)
                    c.hear(dec_ready, 2)
                    for h in range(SSD_H):
                        last = v.tensor_scalar(mix[:, h, :], decay[:, 0, h, :], dt[:, b, h:h + 1], None, ALU.mult)
                    link(last)
                    for h in range(SSD_H):
                        last = v.scalar_tensor_tensor(out=mix[:, h, :], in0=decay[:, 1, h, :],
                                                      scalar=dt[:, b, 4 + h:5 + h], in1=mix[:, h, :],
                                                      op0=ALU.mult, op1=ALU.add)
                    link(last)
                    for g in range(2):
                        o = V.take()
                        V.give(tt(mix[:, 2 * g:2 * g + 2, :], mix[:, 2 * g:2 * g + 2, :], bc_in(o[:, 0:P], 2),
                                  ALU.mult))
                    rs = [r for r in range(2) if FIRST[r] != b]
                    st = WORK[:, 4096:4608].rearrange("p (r h d) -> p r h d", r=2, d=HD)
                    for g in range(2):
                        o = V.take()
                        for r in rs:
                            last = tt(st[:, r, 2 * g:2 * g + 2, :],
                                      o[:, r * P:r * P + P].rearrange("p (h d) -> p h d", d=HD),
                                      bc(ela[:, b, 4 * r + 2 * g:4 * r + 2 * g + 2], HD), ALU.mult)
                        V.give(last)
                    y = y_v[:, b, ATT_W:ATT_W + SSD_W]
                    y4 = y.rearrange("p (h d) -> p h d", d=HD)
                    link(tt(y4, xsb[:, b, 0:256].rearrange("p (h d) -> p h d", d=HD), bc(par("ssd_d"), HD), ALU.mult))
                    for r in rs:
                        link(tt(y4, y4, st[:, r, :, :], ALU.add))
                    o = V.take()
                    V.give(tt(y, y, o[:, 0:256], ALU.add))
                    c.done()
                    link(tt(y, y, tokp[:, b, COL_Z:D], ALU.mult))
                    link(v.tensor_tensor_reduce(out=conv[:, 0, 0:256], in0=y, in1=y, scale=1.0, scalar=0.0,
                                                op0=ALU.mult, op1=ALU.add, accum_out=ssum[:, b:b + 1]))
                mean_sq(ssum[:, 0:nb], SSD_W)
                ask_rsqrt()
                for b in range(nb):
                    y = y_v[:, b, ATT_W:ATT_W + SSD_W]
                    link(v.scalar_tensor_tensor(out=y, in0=y, scalar=srst[:, b:b + 1], in1=par("ssd_norm"),
                                                op0=ALU.mult, op1=ALU.mult))

            def hyena(layer):
                ns = seqs_out(layer)
                nb, n = 2 * ns, SEQ * ns
                dve.wait_ge(a_free, marks["hy", layer])
                for ch in range(6):
                    if ch >= 2:
                        dve.wait_ge(a_full, marks["hturned", layer, ch - 2])
                    o = conv[:, ch % 2, 0:n].rearrange("p (s t) -> p s t", s=ns)
                    c.tell(convolve(o, hyp[:, ch, :, :], ns, lambda i: fcol(layer, F_HW + 6 * i + ch),
                                    fcol(layer, F_HB + ch)), hconv_ready)
                hyu_st = hyu.rearrange("p (s t) d -> p s t d", t=2)
                y_st = y_v.rearrange("p (s t) d -> p s t d", t=2)

                def s2(x):
                    return x.rearrange("p (s d) -> p s d", s=ns)

                ta, tb = s2(conv[:, 0, 0:n]), s2(conv[:, 1, 0:n])
                for order in range(2):
                    for m in range(2):
                        dve.wait_ge(a_free, marks["dft", layer, order, m])
                        kr, ki = [bc_in(spec[:, w, m, 256 * order:256 * order + 256], ns) for w in range(2)]
                        u_r, u_i, y_r, y_i = [s2(x[:, m, 0:n]) for x in (ur, ui, yr, yi)]
                        tt(ta, u_r, kr, ALU.mult)
                        link(tt(tb, u_i, ki, ALU.mult))
                        link(tt(y_r, ta, tb, ALU.subtract))
                        tt(ta, u_r, ki, ALU.mult)
                        link(tt(tb, u_i, kr, ALU.mult))
                        c.tell(tt(y_i, ta, tb, ALU.add), yspec_ready)
                        c.done()
                    bias = bc_in(par("hy_bias")[:, 256 * order:256 * order + 256], ns)
                    for t in range(2):
                        link(tt(ta, hyu_st[:, 0:ns, t, 0:256], bias, ALU.mult))
                        o = V.take()
                        V.give(tt(ta, ta, s2(o[:, 0:n]), ALU.add))
                        c.done()
                        x = hyu_st[:, 0:ns, t, 256 * (order + 1):256 * (order + 2)]
                        if order == 0:
                            c.tell(tt(hyu_st[:, 0:ns, t, 0:256], ta, x, ALU.mult), hz_ready)
                            c.done()
                        else:
                            link(tt(y_st[:, 0:ns, t, 768:1024], ta, x, ALU.mult))
                for b in range(nb):
                    y = y_v[:, b, 768:1024]
                    link(tt(conv[:, 0, 0:256], y, y, ALU.mult))
                    link(v.tensor_reduce(gs[:, b, :], conv[:, 0, 0:256].rearrange("p (g d) -> p g d", g=4), AX_X,
                                         ALU.add))
                mean_sq(gs[:, 0:nb, :], HY_W // HY_GROUPS)
                ask_rsqrt()
                for b in range(nb):
                    y = y_v[:, b, 768:1024]
                    y4 = y.rearrange("p (g d) -> p g d", g=4)
                    link(tt(y4, y4, bc(grst[:, b, :], HD), ALU.mult))
                    ins = tt(y, y, par("hy_out_norm"), ALU.mult)
                    if b < nb - 1:
                        link(ins)
                    else:
                        c.tell(ins, y_ready)

            def output(layer):
                for b in blocks_out(layer):
                    o = V.take()
                    V.give(v.tensor_copy(ht[:, 4:8, b * P:b * P + P], o[:, :].rearrange("p (k t) -> p k t", k=4)))
                for half in range(2):
                    for b in blocks_out(layer):
                        lo = half * 512
                        o = V.take()
                        V.give(tt(conv[:, 0, :], o[:, :], gate[:, 0, b // 2, lo:lo + 512], ALU.mult))
                        c.done()
                        x = x_v[:, b, lo:lo + 512]
                        ins = tt(x, x, conv[:, 0, :], ALU.add)
                        if half == 1 and b == len(blocks_out(layer)) - 1:
                            c.tell(ins, x_ready)
                        else:
                            link(ins)
                c.done()

            def route():
                o = V.take()
                V.give(v.tensor_copy(logit, o[:, 0:16].rearrange("p (b e) -> p b e", b=2)))
                c.done()
                rank = bc_in(con("rank8"), 2)
                for w in range(2):
                    mx, key = top[:, 2 * w, :], top[:, 2 * w + 1, :]
                    link(v.tensor_reduce(mx, logit, AX_X, ALU.max))
                    link(tt(eq, logit, bc(mx, NE), ALU.is_equal))
                    link(tt(eq, eq, rank, ALU.mult))
                    link(v.tensor_reduce(key, eq, AX_X, ALU.max))
                    link(tt(hot[:, w, :, :], eq, bc(key, NE), ALU.is_equal))
                    if w == 0:
                        link(v.scalar_tensor_tensor(out=logit, in0=hot[:, 0, :, :], scalar=-3.0e38, in1=logit,
                                                    op0=ALU.mult, op1=ALU.add))
                c.tell(tt(sel, hot[:, 0, :, :], hot[:, 1, :, :], ALU.add), sel_ready)
                c.tell(tt(top[:, 2, :], top[:, 2, :], top[:, 0, :], ALU.subtract), act_asked)
                c.hear(act_did)
                link(v.tensor_scalar(top[:, 3, :], top[:, 2, :], 1.0, None, ALU.add))
                link(v.reciprocal(top[:, 0, :], top[:, 3, :]))
                link(tt(top[:, 1, :], top[:, 2, :], top[:, 0, :], ALU.mult))
                link(tt(comb, hot[:, 0, :, :], bc(top[:, 0, :], NE), ALU.mult))
                link(tt(eq, hot[:, 1, :, :], bc(top[:, 1, :], NE), ALU.mult))
                link(tt(comb, comb, eq, ALU.add))
                o = V.take()
                far = 1.0e4
                link(v.tensor_scalar(pos, sel, -(1.0 + far), far, ALU.mult, ALU.add))
                link(tt(pos, pos, o[:, 0:16].rearrange("p (b e) -> p b e", b=2), ALU.add))
                V.give(v.tensor_scalar(over, o[:, 16:24], float(P), None, ALU.is_gt))
                c.done()

            def build_gather(j, e, shift):
                if isinstance(j, int) and j == 0:
                    pass
                else:
                    dve.wait_ge(gt_full, j)
                v.tensor_scalar(pe_col, pos[:, :, bass.ds(e, 1)].rearrange("p b e -> p (b e)"), shift, None, ALU.add
                                ).then_inc(col_ready, 1)
                dve.wait_ge(col_ready, j + 1)
                for b in range(2):
                    last = v.tensor_scalar(gm[:, b, :], con("iota"), pe_col[:, b:b + 1], None, ALU.is_equal)
                last.then_inc(g_ready, 1)

            def expert_job(j, e, has_next):
                for s in range(STEPS):
                    dve.wait_ge(sg_ready, j * STEPS + (FFN_HALVES + s + 1))
                    tt(av[0], sg[0], bank[2 + s % 2][:, FSTEP:2 * FSTEP], ALU.mult).then_inc(a_ready, 1)
                    if s == 1 and has_next:
                        build_gather(j + 1, e + 1, 0.0)
                    if s == 2:
                        v.tensor_copy(ce, comb[:, :, bass.ds(e, 1)].rearrange("p b e -> p (b e)")
                                      ).then_inc(ce_ready, 1)
                dve.wait_ge(slot_used, j * STEPS + (3 * STEPS + SLOTS))
                v.tensor_copy(ye[:, 512:1024], bank[1][:, :]).then_inc(ye_ready, 1)
                dve.wait_ge(ce_ready, j + 1)
                dve.wait_ge(s_free, j * 4 + 1)
                for i in range(4):
                    dve.wait_ge(s_full, j * 4 + (i + 1))
                    y = y_v[:, i, 0:512]
                    v.scalar_tensor_tensor(out=y, in0=bank[5 + i % 3][:, :], scalar=ce[:, i // 2:i // 2 + 1],
                                           in1=y, op0=ALU.mult, op1=ALU.add).then_inc(s_free, 1)

            def gated(J):
                for s in range(STEPS):
                    n = (J * STEPS + s) * 2
                    for b in range(2):
                        dve.wait_ge(sg_ready, n + b + 1)
                        tt(av[b], sg[b], bank[4 + b][:, FSTEP:2 * FSTEP], ALU.mult).then_inc(a_ready, 1)

            for layer in range(DEPTH):
                if layer == 0:
                    dve.wait_ge(const_in, 16)
                    dve.wait_ge(feat_in, 16)
                    dve.wait_ge(x_in, 32)
                filters(layer)
                modulation(layer)
                norm(range(NB), 0)
                projections(layer)
                attention(layer)
                ssd(layer)
                hyena(layer)
                output(layer)
                norm(blocks_out(layer), 2)
                if layer == 0:
                    for J in range(2):
                        gated(J)
                        dve.wait_ge(slot_used, (J + 1) * STEPS + SLOTS)
                        for i in range(4):
                            last = tt(y_v[:, i, 0:512], bank[i][:, :],
                                      gate[:, 1, J, 512 * (i % 2):512 * (i % 2) + 512], ALU.mult)
                        c.tell(last, sum_free)
                        c.done()
                        for i in range(4):
                            x = x_v[:, 2 * J + i // 2, 512 * (i % 2):512 * (i % 2) + 512]
                            last = tt(x, x, y_v[:, i, 0:512], ALU.add)
                        if J == 1:
                            c.tell(last, layer_done)
                            c.done()
                        else:
                            link(last)
                else:
                    route()
                    build_gather(0, 0, 0.0)
                    v.memset(y_v[:, :, 0:512], 0.0).then_inc(s_free, 1)
                    link(v.memset(before[:, 0:1], float(NE)))
                    for e in range(1, NE):
                        link(tt(before[:, e:e + 1], before[:, e - 1:e], over[:, e - 1:e], ALU.add))
                    tab = table[:, 0:2 * NE].rearrange("p (e w) -> p e w", w=2)
                    link(v.tensor_copy(tab[:, :, 0], over))
                    link(tt(pe_col[:, 0:1], before[:, NE - 1:NE], over[:, NE - 1:NE], ALU.add))
                    link(v.tensor_copy(table[:, 2 * NE:2 * NE + 1], pe_col[:, 0:1]))
                    c.tell(v.tensor_copy(tab[:, :, 1], before), table_ready)
                    with dve.Fori(0, NE - 1) as e:
                        expert_job(e, e, True)
                    expert_job(NE - 1, NE - 1, False)
                    with dve.Fori(0, NE) as e:
                        again, n = second_turn(dve, e)
                        with dve.If(again):
                            build_gather(n, e, -float(P))
                            expert_job(n, e, False)
                    jobs = dve.value_load(table[0:1, 2 * NE:2 * NE + 1], min_val=NE, max_val=2 * NE)
                    dve.wait_ge(s_free, jobs * 4 + 1)
                    for i in range(4):
                        last = tt(y_v[:, i, 0:512], y_v[:, i, 0:512],
                                  gate[:, 1, 0, 512 * (i % 2):512 * (i % 2) + 512], ALU.mult)
                    link(last)
                    for i in range(4):
                        x = x_v[:, i // 2, 512 * (i % 2):512 * (i % 2) + 512]
                        last = tt(x, x, y_v[:, i, 0:512], ALU.add)
                    c.tell(last, layer_done)


INV_2PI = 1.0 / (2.0 * math.pi)
ROUND = 1.5 * 2.0 ** 23
TWO_PI = (6.28125, 2.0 * math.pi - 6.28125)
PI_F = 3.1415925


_BIG = ["x", "ctx", "w_ada", "b_ada", "w_in", "w_out", "hy_w1", "hy_w2", "hy_w3", "ffn_w_gate", "ffn_w_up",
        "ffn_w_down", "moe_router", "moe_w_gate", "moe_w_up", "moe_w_down"]


def constants():
    import numpy as np
    c = np.zeros((P, CON_COLS), np.float32)
    filt = np.zeros((P, FILT_COLS), np.float32)

    def put(name, a):
        a = np.asarray(a, np.float64).astype(np.float32)
        to, lo = (c, CON[name][0]) if name in CON else (filt, FILT[name][0])
        to[0:a.shape[0], lo:lo + a.shape[1]] = a

    i, j = np.arange(P)[:, None], np.arange(P)[None, :]
    put("ident", i == j)
    put("tri_f", i <= j)
    put("tri_r", i >= j)
    put("neg_f", np.where(i <= j, 0.0, NEG))
    put("neg_r", np.where(i >= j, 0.0, NEG))
    k = np.arange(SEQ)[None, :]
    z = np.zeros((P, SEQ))
    put("mask", np.concatenate([np.where(abs(k - i) <= WINDOW, 0.0, NEG), z,
                                np.where(abs(k - i - P) <= WINDOW, 0.0, NEG), z], axis=1))
    f32 = np.float32
    inv = (f32(10000.0) ** (-np.arange(0, 32, 2, dtype=f32) / f32(32))).astype(f32)
    t = np.arange(SEQ)
    ang = np.stack([(t // 64).astype(f32)[:, None] * inv, (t % 64).astype(f32)[:, None] * inv], axis=1)
    for name, fn in (("cos", np.cos), ("sin", np.sin)):
        put(name, fn(ang.astype(np.float64)).reshape(2, P, 32).transpose(1, 0, 2).reshape(P, 64))
    m, f = np.arange(SEQ)[:, None], np.arange(SEQ)[None, :]
    theta = math.pi * ((2 * f + 1) * m % (4 * SEQ)) / (2 * SEQ)

    def chunks(a):
        return a.reshape(2, P, -1).transpose(1, 0, 2).reshape(P, -1)
    put("dft_c", chunks(np.cos(theta)))
    put("dft_s", chunks(np.sin(theta)))
    put("inv_c", chunks(np.cos(theta).T / SEQ))
    put("inv_s", chunks(np.sin(theta).T / SEQ))
    tl = np.linspace(0.0, 1.0, SEQ)[:, None]
    deltas = abs(np.linspace(math.log(1e-2) / 1.5, math.log(1e-2) / 0.3, HY_W))
    dec = np.exp(-tl * deltas)
    put("decay0", chunks(dec))
    put("decay1", chunks(np.where(m == 0, 0.0, dec)))
    put("ones", np.ones((P, P)))
    put("iota", np.broadcast_to(np.arange(P), (P, P)))
    put("rank8", np.broadcast_to(NE - np.arange(NE), (P, NE)))
    w = (2.0 * math.pi / SEQ) * np.arange(SEQ)[:, None]
    freqs = np.linspace(1e-4, 15, 16)[None, :]
    put("pos", np.concatenate([tl, np.cos(freqs * w), -np.sin(freqs * w)], axis=1).T)
    put("sel", np.concatenate([np.broadcast_to((i[0:2] == s), (2, P)) for s in range(2)], axis=1))
    return c, filt


def kernel(**inputs):
    import numpy as np
    import concourse.bacc as bacc
    from concourse.bass_utils import run_bass_kernel_spmd

    a = {k: np.ascontiguousarray(v) for k, v in inputs.items()}
    cols = []
    for l in range(DEPTH):
        cols += [a["norm1"][l].reshape(8, P), a["norm2"][l].reshape(8, P), a["ssd_conv_w"][l].reshape(12, P),
                 a["ssd_conv_b"][l].reshape(4, P), a["hy_conv_w"][l].reshape(18, P), a["hy_conv_b"][l].reshape(6, P)]
    cols += [a["c"].reshape(8, P), a["c_ctx"].reshape(8, P)]
    data = {n: a[n] for n in _BIG}
    data["feat"] = np.ascontiguousarray(np.concatenate(cols, axis=0).T)
    data["params"] = np.concatenate([a[n].reshape(DEPTH, -1) for n, _ in PARTS], axis=1)
    data["hy_bf"] = np.ascontiguousarray(np.concatenate(
        [a[n][l][:, None] for l in range(DEPTH) for n in ("hy_b1", "hy_f1", "hy_b2", "hy_f2")], axis=1))
    data["const"], data["filter_const"] = constants()

    nc = bacc.Bacc("TRN2", target_bir_lowering=False, num_devices=1)
    arrays, views = {}, {}
    for name, v in data.items():
        arrays[f"in_{name}"] = v
        views[name] = nc.dram_tensor(f"in_{name}", v.shape, mybir.dt.from_np(v.dtype), kind="ExternalInput").ap()
    out = nc.dram_tensor("out_x", (1, SEQ, D), F32, kind="ExternalOutput").ap()
    hybrid_block(nc, views, out)
    r = run_bass_kernel_spmd(nc, [arrays], core_ids=[0])
    return r.results[0]["out_x"]
```

```python
import math
from contextlib import ExitStack

import concourse.bass as bass
from concourse import mybir

F32 = mybir.dt.float32
ALU = mybir.AluOpType
ACT = mybir.ActivationFunctionType
AX_X = mybir.AxisListType.X

P = 128
D = 1024
KD = D // P
SEQ = 256
NTOK = 2 * SEQ
NB = NTOK // P
DEPTH = 2
HEADS, KV_HEADS, HD = 8, 2, 64
GROUP = HEADS // KV_HEADS
WINDOW = 128
ATT_W = HEADS * HD
SSD_W, SSD_H = 256, 4
HY_W, HY_GROUPS = 256, 4
XBC = 512
COL_Q, COL_K, COL_V, COL_Z = 0, 512, 640, 768
COL_XBC, COL_DT, COL_HY, PROJ = 1024, 1536, 1544, 2312
FFN = 2816
NE = 8
EPS = 1e-6
FSTEP = 256
SLOTS = 3
UNITS = [FSTEP] * (FFN // FSTEP - 1) + [FSTEP // 2] * 2
STEPS = len(UNITS)
SLOT_USES = STEPS // SLOTS
assert sum(UNITS) == FFN and STEPS % SLOTS == 0
NEG = -1.0e30

F_N1, F_N2, F_SW, F_SB, F_HW, F_HB, F_BA, F_LAYER = 0, 8, 16, 28, 32, 50, 56, 88
F_C = DEPTH * F_LAYER
F_COLS = F_C + 16

PARTS = [("q_norm", 64), ("k_norm", 64), ("att_sinks", 8), ("att_out_norm", 512), ("ssd_dt_bias", 8),
         ("ssd_a_log", 8), ("ssd_d", 4), ("ssd_norm", 256), ("hy_bias", 512), ("hy_out_norm", 256)]
PAR, PAR_COLS = {}, 0
for _name, _n in PARTS:
    PAR[_name] = (PAR_COLS, PAR_COLS + _n)
    PAR_COLS += _n

CPARTS = [("ident", P), ("tri_f", P), ("tri_r", P), ("neg_f", P), ("neg_r", P), ("mask", 4 * SEQ),
          ("cos", 2 * 32), ("sin", 2 * 32), ("dft_c", 512), ("dft_s", 512), ("inv_c", 512), ("inv_s", 512),
          ("ones", P), ("iota", P), ("rank8", 8), ("gsel", 256)]
FILT_PARTS = [("decay0", 512), ("decay1", 512), ("pos", SEQ)]
CON, CON_COLS = {}, 0
for _name, _n in CPARTS:
    CON[_name] = (CON_COLS, CON_COLS + _n)
    CON_COLS += _n
FILT, FILT_COLS = {}, 0
for _name, _n in FILT_PARTS:
    FILT[_name] = (FILT_COLS, FILT_COLS + _n)
    FILT_COLS += _n


class Counts:

    def __init__(self, eng, own):
        self.eng, self.own, self.told, self.heard, self.last = eng, own, {}, {}, None

    def tell(self, ins, sem):
        ins.then_inc(sem, 1)
        self.told[sem] = self.told.get(sem, 0) + 1
        self.last = (sem, self.told[sem])

    def done(self):
        self.eng.wait_ge(*self.last)

    def link(self, ins):
        self.tell(ins, self.own)
        self.done()

    def hear(self, sem, k=1):
        self.heard[sem] = self.heard.get(sem, 0) + k
        self.eng.wait_ge(sem, self.heard[sem])


class Ring:

    def __init__(self, counts, banks, full, free):
        self.c, self.banks, self.full, self.free, self.n = counts, banks, full, free, 0

    def bank(self):
        return self.banks[self.n % len(self.banks)]

    def open(self):
        b = self.bank()
        if self.n >= len(self.banks):
            self.c.eng.wait_ge(self.free, self.n - len(self.banks) + 1)
        self.n += 1
        return b

    def close(self, ins):
        ins.then_inc(self.full, 1)

    def drained(self):
        self.c.eng.wait_ge(self.free, self.n)

    def take(self):
        b = self.bank()
        self.n += 1
        self.c.eng.wait_ge(self.full, self.n)
        return b

    def give(self, ins):
        self.c.tell(ins, self.free)


def hybrid_block(nc, A, out):
    with ExitStack() as ctx:
        def sb(name, cols):
            return ctx.enter_context(nc.sbuf_tensor(name, [P, cols], F32))

        def sem(name):
            return ctx.enter_context(nc.semaphore(name))

        bank = [ctx.enter_context(nc.psum_tensor(f"bank{i}", [P, 512], F32)) for i in range(8)]
        V_BANKS, A_BANKS, O_BANKS = bank[0:3], bank[3:6], bank[6:8]

        ring = sb("ring", SLOTS * 6144)
        const = sb("const", CON_COLS)
        feat = sb("feat", F_COLS)
        params = sb("params", PAR_COLS)
        X = sb("X", NB * D)
        GATE = sb("GATE", 4 * D)
        HTY = sb("HTY", KD * NTOK + NB * D)
        HT, Y = HTY[:, 0:KD * NTOK], HTY[:, KD * NTOK:KD * NTOK + NB * D]
        HYE = sb("HYE", 3072)
        XBCS = sb("XBCS", 2048)
        WORK = sb("WORK", 5632)
        small = sb("small", 1330)

        x_v = X[:, :].rearrange("p (b d) -> p b d", b=NB)
        ht = HT.rearrange("p (k t) -> p k t", k=KD)
        gates = [GATE[:, :].rearrange("p (g s d) -> p g s d", g=2, s=2),
                 GATE[:, 0:2 * D].rearrange("p (g s d) -> p g s d", g=2, s=1)]
        y_v = Y.rearrange("p (b d) -> p b d", b=NB)
        wslot = [ring[:, i * 4096:(i + 1) * 4096] for i in range(2)]
        tokp = ring[:, 8192:12288].rearrange("p (b d) -> p b d", b=NB)
        xbcp = ring[:, 12288:14352].rearrange("p (c s t) -> p c s t", c=4, s=2)
        hyp = ring[:, 14352:17448].rearrange("p (c s t) -> p c s t", c=6, s=2)
        ada = HT[:, 0:1024].rearrange("p (i d) -> p i d", i=2)
        hyu = WORK[:, 0:3072].rearrange("p (b d) -> p b d", b=NB)
        spec = HYE[:, 0:2048].rearrange("p (r m d) -> p r m d", r=2, m=2)
        conv = HYE[:, 2048:3072].rearrange("p (i d) -> p i d", i=2)
        xbcs = XBCS[:, :].rearrange("p (c t) -> p c t", c=4)
        xsb = ring[:, 12288:12288 + 4 * 384].rearrange("p (b d) -> p b d", b=NB)
        qt = WORK[:, 0:2048].rearrange("p (j t) -> p j t", j=4)
        kt = WORK[:, 2048:2560]
        sc = WORK[:, 2560:3584].rearrange("p (i d) -> p i d", i=2)
        pr = WORK[:, 3584:4608].rearrange("p (i d) -> p i d", i=2)
        pt = WORK[:, 4608:5632].rearrange("p (i d) -> p i d", i=2)
        qn = WORK[:, 2560:3200]
        rope_a = WORK[:, 3200:3520]
        rope_b = WORK[:, 3520:3840]
        qr = WORK[:, 3840:5120].rearrange("p (i d) -> p i d", i=2)
        xn = WORK[:, 0:4096].rearrange("p (b d) -> p b d", b=NB)
        junk = WORK[:, 4096:5120]
        hin = WORK[:, 0:2048].rearrange("p (r b d) -> p r b d", r=2, b=NB)
        decay = WORK[:, 2048:3072].rearrange("p (r h l) -> p r h l", r=2, h=4)
        mix = WORK[:, 3072:3584].rearrange("p (h l) -> p h l", h=4)
        xw = WORK[:, 3584:4096].rearrange("p (r d) -> p r d", r=2)
        ssdt = WORK[:, 4096:5120].rearrange("p (i d) -> p i d", i=4)
        ssdy = WORK[:, 5120:5632].rearrange("p (i d) -> p i d", i=2)
        ur = HT[:, 0:1024].rearrange("p (m d) -> p m d", m=2)
        ui = HT[:, 1024:2048].rearrange("p (m d) -> p m d", m=2)
        yr = HT[:, 2048:3072].rearrange("p (m d) -> p m d", m=2)
        yi = HT[:, 3072:4096].rearrange("p (m d) -> p m d", m=2)
        fw1 = WORK[0:33, 0:64]
        fw2 = WORK[0:64, 64:128]
        fw3 = WORK[0:64, 128:1152]
        fbf = WORK[0:64, 1152:1156]
        farg = WORK[0:64, 1280:1536]
        fk = WORK[0:64, 1536:1792]
        fh = [WORK[0:64, 1792:2048], WORK[0:64, 2048:2304]]
        fp = WORK[:, 2304:3328].rearrange("p (t d) -> p t d", t=2)
        fq = WORK[:, 3328:4352].rearrange("p (t d) -> p t d", t=2)
        fd = [ring[:, 8192:8704], ring[:, 8704:9216]]
        h2 = WORK[:, 0:2048].rearrange("p (b d) -> p b d", b=2)
        xe = WORK[:, 2048:3072].rearrange("p (k r) -> p k r", k=KD)
        gm = WORK[:, 3072:3328].rearrange("p (b r) -> p b r", b=2)
        gt = WORK[:, 3328:3584]
        ye = WORK[:, 3584:4608]
        sg = [XBCS[:, 256 * b:256 * b + 256] for b in range(2)]
        av = [XBCS[:, 512 + 256 * b:768 + 256 * b] for b in range(2)]
        at = [XBCS[:, 1024 + 256 * b:1280 + 256 * b].rearrange("p (f t) -> p f t", f=2) for b in range(2)]

        used = [0]

        def sm(n):
            used[0] += n
            assert used[0] <= 1330
            return small[:, used[0] - n:used[0]]

        silu_c = sm(256).rearrange("p (k s) -> p k s", s=32)
        coefs = [sm(64).rearrange("p (w k s) -> p w k s", w=4, s=2) for _ in range(DEPTH)]
        ssum, srst = sm(8), sm(8)
        qsum, qrst = sm(40).rearrange("p (b h) -> p b h", b=NB), sm(40).rearrange("p (b h) -> p b h", b=NB)
        rawm, negm, psumr = [sm(16).rearrange("p (i h) -> p i h", i=2) for _ in range(3)]
        qgain = sm(64)
        mhalf = sm(64)
        rden = sm(8)
        snk = sm(8)
        dtu = sm(32).rearrange("p (b h) -> p b h", b=NB)
        dte = sm(32).rearrange("p (b h) -> p b h", b=NB)
        dt = sm(32).rearrange("p (b h) -> p b h", b=NB)
        dta = sm(32).rearrange("p (b h) -> p b h", b=NB)
        aexp = sm(8)
        la = sm(64).rearrange("p (b h) -> p b h", b=NB)
        wend = sm(32).rearrange("p (b h) -> p b h", b=NB)
        ela = sm(64).rearrange("p (b h) -> p b h", b=NB)
        gs, grst = sm(16).rearrange("p (b h) -> p b h", b=NB), sm(16).rearrange("p (b h) -> p b h", b=NB)
        logit = sm(16).rearrange("p (b e) -> p b e", b=2)
        eq = sm(16).rearrange("p (b e) -> p b e", b=2)
        top = sm(8).rearrange("p (w b) -> p w b", w=4)
        hot = sm(32).rearrange("p (w b e) -> p w b e", w=2, b=2)
        sel = sm(16).rearrange("p (b e) -> p b e", b=2)
        pos = sm(16).rearrange("p (b e) -> p b e", b=2)
        over, before = sm(8), sm(8)
        pe_col = sm(2)
        few, many = logit[:, 0, :], logit[:, 1, :]
        comb = sm(16).rearrange("p (b e) -> p b e", b=2)
        ce = sm(2)
        router = sm(KD * NE).rearrange("p (k e) -> p k e", k=KD)

        fconst = ring[:, 9216:9216 + FILT_COLS]

        def fcon(name):
            return fconst[:, FILT[name][0]:FILT[name][1]]

        table = ctx.enter_context(nc.sbuf_tensor("table", [P, 4 * NE + 1], mybir.dt.int32))

        def con(name):
            return const[:, CON[name][0]:CON[name][1]]

        def par(name):
            return params[:, PAR[name][0]:PAR[name][1]]

        ident = con("ident")
        dft = {n: con(n).rearrange("p (t f) -> p t f", t=2) for n in ("dft_c", "dft_s", "inv_c", "inv_s")}

        const_in, feat_in, x_in, par_in, b_in = sem("const_in"), sem("feat_in"), sem("x_in"), sem("par_in"), sem("b_in")
        filt_in, router_in, out_done = sem("filt_in"), sem("router_in"), sem("out_done")
        tile_in = [sem("tile_loaded0"), sem("tile_loaded1")]
        slot_in = [sem(f"slot_loaded{i}") for i in range(SLOTS)]
        slot_used = sem("slot_used")
        v_full, v_free, a_full, a_free = sem("v_full"), sem("v_free"), sem("a_full"), sem("a_free")
        vec_own, act_own, pool_own = sem("vec_own"), sem("act_own"), sem("pool_own")
        silu_c_ready, zeros_ready, coef_ready = sem("silu_c_ready"), sem("zeros_ready"), sem("coef_ready")
        sq_ready, pow_asked, pow_ready, xn_ready = sem("sq_ready"), sem("pow_asked"), sem("pow_ready"), sem("xn_ready")
        pads_ready, arg_ready, sin_ready, fpq_ready = (
            sem("pads_ready"), sem("arg_ready"), sem("sin_ready"), sem("fpq_ready"))
        qr_ready, sc_ready, p_ready, o_full, o_free = (
            sem("qr_ready"), sem("sc_ready"), sem("p_ready"), sem("o_full"), sem("o_free"))
        act_asked, act_did = sem("act_asked"), sem("act_did")
        conv_ready, xbc_ready, zs_ready, dta_ready = (
            sem("conv_ready"), sem("xbc_ready"), sem("zs_ready"), sem("dta_ready"))
        dec_ready, xw_ready, h_ready = sem("dec_ready"), sem("xw_ready"), sem("h_ready")
        hconv_ready, hz_ready, yspec_ready = sem("hconv_ready"), sem("hz_ready"), sem("yspec_ready")
        y_ready, x_ready = sem("y_ready"), sem("x_ready")
        gu_full, sg_ready, a_ready, t_full, at_ready, sum_free, ce_ready = (
            sem("gu_full"), sem("sg_ready"), sem("a_ready"), sem("t_full"), sem("at_ready"), sem("sum_free"),
            sem("ce_ready"))
        sel_ready, table_ready, col_ready = sem("sel_ready"), sem("table_ready"), sem("col_ready")
        g_ready, xe_full, xe_ready, gt_full, gt_ready, ye_ready, s_full, s_free = (
            sem("g_ready"), sem("xe_full"), sem("xe_ready"), sem("gt_full"), sem("gt_ready"), sem("ye_ready"),
            sem("s_full"), sem("s_free"))
        layer_done = sem("layer_done")
        FFN_HALVES = 2 * 2 * STEPS

        IN_TILES = [(0, 512), (512, 1024), (1024, 1536), (1536, 1544 + 384), (1544 + 384, 2312)]
        COLUMN_TILES, GATE_TILES = [0, 1, 2, 3, 6, 7, 8, 9], [4, 5, 10, 11]
        COEF_OF = {0: 0, 1: 1, 3: 2, 4: 3}
        STAGE_AFTER_TILE, STAGE_AFTER_PRODUCT = {1: 0, 3: 1, 5: 2, 7: 3}, {0: 0, 2: 1, 4: 2, 6: 3}

        def tiles(layer):
            if layer == 0:
                for t in COLUMN_TILES + GATE_TILES:
                    yield ada_src(layer, t)
            for lo, hi in IN_TILES:
                yield A["w_in"][layer, :, lo:hi], hi - lo
            if layer + 1 < DEPTH:
                for t in COLUMN_TILES:
                    yield ada_src(layer + 1, t)
            for t in range(2):
                yield A["w_out"][layer, :, 512 * t:512 * t + 512], 512
            if layer + 1 < DEPTH:
                for t in GATE_TILES:
                    yield ada_src(layer + 1, t)

        def ada_src(layer, t):
            return A["w_ada"][layer, :, 512 * t:512 * t + 512], 512

        def tile_view(i, n):
            return wslot[i][:, 0:KD * n].rearrange("p (k n) -> p k n", k=KD)

        def slot_views(s):
            base = ring[:, s * 6144:(s + 1) * 6144]
            return (base[:, 0:4096].rearrange("p (k w f) -> p k w f", k=KD, w=2),
                    base[:, 4096:6144].rearrange("p (f d) -> p f d", f=2))

        def second_turn(eng, e):
            again = eng.value_load(table[0:1, bass.ds(e * 4, 1)], min_val=0, max_val=1)
            n = eng.value_load(table[0:1, bass.ds(e * 4 + 1, 1)], min_val=NE, max_val=2 * NE)
            return again, n

        def by_size(eng, e, job):
            few = eng.value_load(table[0:1, bass.ds(e * 4 + 2, 1)], min_val=0, max_val=1)
            many = eng.value_load(table[0:1, bass.ds(e * 4 + 3, 1)], min_val=0, max_val=1)
            with eng.If(few):
                job(True)
            with eng.If(many):
                job(False)

        tile_done = []
        marks = {}

        def blocks_out(layer):
            return range(NB) if layer < DEPTH - 1 else range(2)

        def seqs_out(layer):
            return len(blocks_out(layer)) // 2

        def units(layer):
            return [(b, h) for b in blocks_out(layer) for h in range(HEADS)]

        def keys_of(b):
            return (0, NTOK) if b < 2 else (SEQ, NTOK)

        def bc(ap, n):
            return ap.unsqueeze(len(ap.shape)).broadcast_to(list(ap.shape) + [n])

        def bc_in(ap, n):
            return ap.unsqueeze(1).broadcast_to([ap.shape[0], n] + list(ap.shape[1:]))

        ADA_EVERY = 3
        gsel = con("gsel").rearrange("p (s d) -> p s d", s=2)

        FWD_NEXT = {2: 3, 3: 0, 0: 1}
        REV_NEXT = {3: 2, 2: 1, 1: 0}
        NEXT = [FWD_NEXT, REV_NEXT]
        FIRST = [2, 3]

        block = ctx.enter_context(nc.Block())

        @block.tensor
        def _(pe):
            c = Counts(pe, None)
            V = Ring(c, V_BANKS, v_full, v_free)
            S = Ring(c, A_BANKS, a_full, a_free)
            tile_no = [0]

            def mm(o, lhsT, rhs, start=True, stop=True):
                return nc.tensor.matmul(o, lhsT, rhs, start=start, stop=stop)

            def tile(n):
                g = tile_no[0]
                tile_no[0] += 1
                pe.wait_ge(tile_in[g % 2], 16 * (g // 2 + 1))
                return tile_view(g % 2, n)

            def tile_ends(r):
                tile_done.append((r.full, r.n))

            def over_k(o, lhsT, rhs):
                for k in range(KD):
                    last = mm(o, lhsT(k), rhs(k), start=(k == 0), stop=(k == KD - 1))
                return last

            def filter_stage(layer, stage):
                if stage == 0:
                    pe.wait_ge(filt_in, 80 * (layer + 1))
                    b = V.open()
                    V.close(mm(b[0:64, 0:SEQ], fw1, fcon("pos")[0:33, :]))
                if stage == 1:
                    c.hear(sin_ready)
                    b = V.open()
                    V.close(mm(b[0:64, 0:SEQ], fw2, fh[0]))
                if stage == 2:
                    c.hear(sin_ready)
                    for t in range(2):
                        for d in range(2):
                            b = V.open()
                            V.close(mm(b[:, :], fh[1][:, t * P:t * P + P], fw3[:, d * 512:d * 512 + 512]))
                if stage == 3:
                    c.hear(fpq_ready)
                    for n, src in (("dft_c", fp), ("dft_s", fq)):
                        for m in range(2):
                            b = S.open()
                            mm(b[:, :], dft[n][:, 0, m * P:m * P + P], src[:, 0, :], True, False)
                            S.close(mm(b[:, :], dft[n][:, 1, m * P:m * P + P], src[:, 1, :], False, True))

            ada_open = []
            ada_no = [0]

            def ada_products(layer, t):
                w = tile(512)
                o = S.open()
                for k in range(KD):
                    g = k % 4
                    last = mm(o[32 * g:32 * g + 32, :], silu_c[:, k, :], w[:, k, :], k < 4, k >= 4)
                S.close(last)
                tile_ends(S)
                ada_open.append((layer, t, S.n, ada_no[0] % 2))
                ada_no[0] += 1

            def ada_sums():
                layer, t, n, i = ada_open.pop(0)
                pe.wait_ge(a_free, n)
                if t in COLUMN_TILES:
                    o = V.open()
                    for q in range(4):
                        last = mm(o[:, 2 * q:2 * q + 2], ada[:, i, q * P:q * P + P], gsel[:, :, 0])
                    V.close(last)
                else:
                    for x in range(gates[layer].shape[2]):
                        o = V.open()
                        V.close(mm(o[:, :], gsel[:, x, :], ada[:, i, :]))

            def modulation(layer, ts):
                for n, t in enumerate(ts):
                    ada_products(layer, t)
                    if len(ada_open) == 2:
                        ada_sums()
                    if layer == 0 and n in STAGE_AFTER_TILE:
                        filter_stage(0, STAGE_AFTER_TILE[n])
                ada_sums()

            def to_features(src, blocks, ready=None):
                for b in blocks:
                    if ready is not None:
                        c.hear(ready)
                    for i, r in enumerate((S, V)):
                        o = r.open()
                        for k in range(4):
                            kk = 4 * i + k
                            last = nc.tensor.transpose(o[:, k * P:k * P + P], src[:, b, kk * P:kk * P + P], ident)
                        r.close(last)

            def projections(layer):
                S.drained()
                V.drained()
                w = tile(512)
                for b in blocks_out(layer):
                    o = V.open()
                    V.close(over_k(o[:, :], lambda k: ht[:, k, b * P:b * P + P], lambda k: w[:, k, :]))
                tile_ends(V)
                w = tile(512)
                for b in range(NB):
                    o = S.open()
                    S.close(over_k(o[:, :], lambda k: ht[:, k, b * P:b * P + P], lambda k: w[:, k, :]))
                tile_ends(S)
                marks["kv", layer] = S.n
                w = tile(512)
                for ch in range(4):
                    o = S.open()
                    S.close(over_k(o[:, :], lambda k: w[:, k, ch * P:ch * P + P], lambda k: ht[:, k, :]))
                tile_ends(S)
                marks["xbc", layer] = S.n
                n = SEQ * seqs_out(layer)
                w = tile(8 + 384)
                o = S.open()
                for b in range(NB):
                    last = over_k(o[:, b * 8:b * 8 + 8], lambda k: ht[:, k, b * P:b * P + P], lambda k: w[:, k, 0:8])
                S.close(last)
                marks["dt", layer] = S.n
                for ch in range(3):
                    o = S.open()
                    S.close(over_k(o[:, 0:n], lambda k: w[:, k, 8 + ch * P:8 + ch * P + P], lambda k: ht[:, k, 0:n]))
                tile_ends(S)
                w = tile(384)
                for ch in range(3):
                    o = S.open()
                    S.close(over_k(o[:, 0:n], lambda k: w[:, k, ch * P:ch * P + P], lambda k: ht[:, k, 0:n]))
                tile_ends(S)
                marks["hy", layer] = S.n

            def attention(layer):
                for b in range(NB):
                    c.hear(qr_ready)
                    q = qr[:, b % 2, :]
                    if b in blocks_out(layer):
                        o = S.open()
                        for j in range(4):
                            last = nc.tensor.transpose(o[:, j * P:j * P + P], q[:, j * P:j * P + P], ident)
                        S.close(last)
                    o = V.open()
                    V.close(nc.tensor.transpose(o[:, 0:P], q[:, 512:640], ident))
                    marks["turned", layer, b] = V.n
                S.drained()
                V.drained()
                us = units(layer)
                turned = {}
                for i in range(len(us) + 2):
                    for n, t in enumerate(COLUMN_TILES if layer + 1 < DEPTH else []):
                        if i == ADA_EVERY * (n + 1):
                            ada_products(layer + 1, t)
                        if i == ADA_EVERY * (n + 1) + 1:
                            ada_sums()
                    if i < len(us):
                        b, h = us[i]
                        g, j = h // GROUP, h % GROUP
                        lo, hi = keys_of(b)
                        o = V.open()
                        V.close(mm(o[:, 0:hi - lo], qt[64 * g:64 * g + 64, j, b * P:b * P + P],
                                   kt[64 * g:64 * g + 64, lo:hi]))
                    if 1 <= i <= len(us):
                        b, h = us[i - 1]
                        lo, hi = keys_of(b)
                        c.hear(p_ready)
                        o = S.open()
                        for x in range((hi - lo) // P):
                            last = nc.tensor.transpose(o[:, x * P:x * P + P], pr[:, (i - 1) % 2, x * P:x * P + P],
                                                       ident)
                        S.close(last)
                        turned[i - 1] = S.n
                    if i >= 2:
                        b, h = us[i - 2]
                        lo, hi = keys_of(b)
                        g, n = h // GROUP, (hi - lo) // P
                        pe.wait_ge(a_free, turned[i - 2])
                        if h == 0 and b >= 2:
                            c.hear(o_free)
                        for x in range(n):
                            kb = lo // P + x
                            last = mm(O_BANKS[b % 2][:, h * HD:h * HD + HD], pt[:, (i - 2) % 2, x * P:x * P + P],
                                      tokp[:, kb, COL_V + g * HD:COL_V + g * HD + HD], x == 0, x == n - 1)
                        if h == HEADS - 1:
                            last.then_inc(o_full, 1)

            def ssd(layer):
                c.hear(xbc_ready, 4)
                for b in range(NB):
                    o = S.open()
                    for ch in range(3):
                        last = nc.tensor.transpose(o[:, ch * P:ch * P + P], xbcs[:, ch, b * P:b * P + P], ident)
                    S.close(last)
                marks["xsb", layer] = S.n
                c.hear(dta_ready)
                o = V.open()
                for b in range(NB):
                    mm(o[:, b * 16:b * 16 + 4], con("tri_f"), dta[:, b, 0:4])
                    mm(o[:, b * 16 + 4:b * 16 + 8], con("tri_r"), dta[:, b, 4:8])
                    last = mm(o[:, b * 16 + 8:b * 16 + 16], con("ones"), dta[:, b, :])
                V.close(last)
                for b in range(NB):
                    c.hear(xw_ready)
                    o = V.open()
                    V.close(mm(o[:, :], xsb[:, b, 256:384], xw[:, :, :]))
                c.hear(h_ready)
                for b in blocks_out(layer):
                    for r, tri in enumerate(("tri_f", "tri_r")):
                        o = V.open()
                        for h in range(SSD_H):
                            last = mm(o[:, h * P:h * P + P],
                                      dta[:, b, r * 4 + h:r * 4 + h + 1].broadcast_to([P, P]), con(tri))
                        V.close(last)
                        marks["seg", layer, b, r] = V.n
                    for g in range(2):
                        o = V.open()
                        V.close(mm(o[:, 0:P], xbcs[64 * g:64 * g + 64, 2, b * P:b * P + P],
                                   xbcs[64 * g:64 * g + 64, 3, b * P:b * P + P]))
                    mixed = V.n
                    rs = [r for r in range(2) if FIRST[r] != b]
                    for g in range(2):
                        o = V.open()
                        for r in rs:
                            last = mm(o[:, r * P:r * P + P], xbcs[64 * g:64 * g + 64, 3, b * P:b * P + P],
                                      hin[64 * g:64 * g + 64, r, b, g * P:g * P + P])
                        V.close(last)
                    pe.wait_ge(v_free, mixed)
                    o = V.open()
                    for h in range(SSD_H):
                        last = mm(o[:, h * HD:h * HD + HD], mix[:, h, :], xsb[:, b, h * HD:h * HD + HD])
                    V.close(last)

            def hyena(layer):
                ns = seqs_out(layer)
                nb, n = 2 * ns, SEQ * ns
                hyu_st = hyu.rearrange("p (s t) d -> p s t d", t=2)
                for ch in range(6):
                    c.hear(hconv_ready)
                    o = S.open()
                    for b in range(nb):
                        last = nc.tensor.transpose(o[:, b * P:b * P + P], conv[:, ch % 2, b * P:b * P + P], ident)
                    S.close(last)
                    marks["hturned", layer, ch] = S.n
                S.drained()
                for order in range(2):
                    if order == 1:
                        c.hear(hz_ready, 2)
                    for m in range(2):
                        for name in ("dft_c", "dft_s"):
                            o = S.open()
                            for t in range(2):
                                last = mm(o[:, 0:n], dft[name][:, t, m * P:m * P + P], hyu_st[:, 0:ns, t, 0:256],
                                          t == 0, t == 1)
                            S.close(last)
                        marks["dft", layer, order, m] = S.n
                    c.hear(yspec_ready, 2)
                    for t in range(2):
                        o = V.open()
                        for m in range(2):
                            mm(o[:, 0:n], dft["inv_c"][:, m, t * P:t * P + P], yr[:, m, 0:n], m == 0, False)
                            last = mm(o[:, 0:n], dft["inv_s"][:, m, t * P:t * P + P], yi[:, m, 0:n], False, m == 1)
                        V.close(last)

            def output(layer):
                c.hear(y_ready)
                to_features(y_v, blocks_out(layer))
                S.drained()
                V.drained()
                for half in range(2):
                    w = tile(512)
                    for b in blocks_out(layer):
                        o = V.open()
                        V.close(over_k(o[:, :], lambda k: ht[:, k, b * P:b * P + P], lambda k: w[:, k, :]))
                        if b == blocks_out(layer)[-1]:
                            tile_ends(V)
                        n = half * NB + b
                        if layer + 1 < DEPTH and n in STAGE_AFTER_PRODUCT:
                            filter_stage(layer + 1, STAGE_AFTER_PRODUCT[n])

            def route():
                pe.wait_ge(router_in, 16)
                o = V.open()
                for b in range(2):
                    last = over_k(o[:, b * NE:b * NE + NE], lambda k: ht[:, k, b * P:b * P + P],
                                  lambda k: router[:, k, :])
                V.close(last)
                for b in range(2):
                    for half in range(2):
                        o = S.open()
                        for k in range(4):
                            last = nc.tensor.transpose(o[:, k * P:k * P + P],
                                                       ht[:, 4 * half + k, b * P:b * P + P], ident)
                        S.close(last)
                c.hear(sel_ready)
                o = V.open()
                mm(o[:, 0:8], con("tri_f"), sel[:, 0, :])
                mm(o[:, 8:16], con("tri_f"), sel[:, 1, :], True, False)
                mm(o[:, 8:16], con("ones"), sel[:, 0, :], False, True)
                mm(o[:, 16:24], con("ones"), sel[:, 0, :], True, False)
                V.close(mm(o[:, 16:24], con("ones"), sel[:, 1, :], False, True))
                V.drained()
                S.drained()

            def gather(j):
                pe.wait_ge(g_ready, j + 1)
                for i in range(2):
                    for k in range(4):
                        for b in range(2):
                            last = mm(bank[5 + i][:, k * P:k * P + P],
                                      h2[:, b, (4 * i + k) * P:(4 * i + k) * P + P], gm[:, b, :], b == 0, b == 1)
                    last.then_inc(xe_full, 1)

            def turn_gather(j):
                pe.wait_ge(s_free, j * 4 + 1)
                for b in range(2):
                    last = nc.tensor.transpose(bank[7][:, b * P:b * P + P], gm[:, b, :], ident)
                last.then_inc(gt_full, 1)

            def expert_job(j, has_last, has_next, few):
                def hidden(s, k0, k1):
                    gu, _ = slot_views(s % SLOTS)
                    o, u = bank[2 + s % 2], UNITS[s]
                    for k in range(k0, k1):
                        if few:
                            for h in range(u // P):
                                last = mm(o[64 * h:64 * h + 64, 0:2 * P], xe[:, k, 0:64],
                                          gu[:, k, :, P * h:P * h + P], k == 0, k == KD - 1)
                        else:
                            last = mm(o[:, 0:2 * u], xe[:, k, :], gu[:, k, :, 0:u], k == 0, k == KD - 1)
                    if k1 == KD:
                        last.then_inc(gu_full, 1)

                def turn(s):
                    pe.wait_ge(a_ready, j * STEPS + (FFN_HALVES + s + 1))
                    for f in range(1 if few else UNITS[s] // P):
                        last = nc.tensor.transpose(bank[4][:, f * P:f * P + P], av[0][:, f * P:f * P + P], ident)
                    last.then_inc(t_full, 1)

                def down(s):
                    _, dn = slot_views(s % SLOTS)
                    pe.wait_ge(at_ready, j * STEPS + (FFN_HALVES + s + 1))
                    for f in range(UNITS[s] // P):
                        begin, end = s == 0 and f == 0, s == STEPS - 1
                        for half in range(2):
                            w = dn[:, f, half * 512:half * 512 + 512]
                            if few:
                                last = mm(bank[half][64 * half:64 * half + 64, :], at[0][:, 0, 64 * f:64 * f + 64], w,
                                          begin, end)
                            else:
                                last = mm(bank[half][:, :], at[0][:, f, :], w, begin, end)
                    last.then_inc(slot_used, 1)

                pe.wait_ge(xe_ready, j * 2 + 2)
                for s in range(STEPS):
                    i = s % SLOTS
                    pe.wait_ge(slot_in[i], j * (SLOT_USES * 48) + (2 * SLOT_USES + s // SLOTS + 1) * 48)
                    hidden(s, 0, 4)
                    if s:
                        turn(s - 1)
                    hidden(s, 4, KD)
                    if s:
                        down(s - 1)
                    elif has_last:
                        put_back(j, 1)
                    if s == 2:
                        turn_gather(j)
                if has_next:
                    gather(j + 1)
                turn(STEPS - 1)
                down(STEPS - 1)

            def put_back(j, ago=0):
                pe.wait_ge(ye_ready, j * 2 + (2 - 2 * ago))
                pe.wait_ge(gt_ready, j + (1 - ago))
                for i in range(4):
                    if i == 3:
                        pe.wait_ge(s_free, j * 4 + (2 - 4 * ago))
                    t, half = i // 2, i % 2
                    mm(bank[5 + i % 3][:, :], gt[:, t * P:t * P + P], ye[:, half * 512:half * 512 + 512]
                       ).then_inc(s_full, 1)

            def ffn_job(J, b0, first):
                def hidden(b, k0, k1):
                    for k in range(k0, k1):
                        last = mm(bank[4 + b][:, 0:2 * u], ht[:, k, (b0 + b) * P:(b0 + b) * P + P],
                                  gu[:, k, :, 0:u], k == 0, k == KD - 1)
                    if k1 == KD:
                        last.then_inc(gu_full, 1)

                def turn(b):
                    pe.wait_ge(a_ready, n + b + 1)
                    for f in range(u // P):
                        last = nc.tensor.transpose(bank[6 + b][:, f * P:f * P + P], av[b][:, f * P:f * P + P], ident)
                    last.then_inc(t_full, 1)

                def down(b, parts):
                    for f, half in parts:
                        last = mm(bank[2 * b + half][:, :], at[b][:, f, :], dn[:, f, half * 512:half * 512 + 512],
                                  s == 0 and f == 0, s == STEPS - 1)
                    return last

                for s in range(STEPS):
                    gu, dn = slot_views(s % SLOTS)
                    u = UNITS[s]
                    parts = [(f, half) for f in range(u // P) for half in range(2)]
                    n = (J * STEPS + s) * 2
                    pe.wait_ge(slot_in[s % SLOTS], (J * SLOT_USES + s // SLOTS + 1) * 48)
                    hidden(0, 0, KD)
                    hidden(1, 0, 4)
                    turn(0)
                    hidden(1, 4, KD)
                    if s == 0 and not first:
                        pe.wait_ge(sum_free, J)
                    pe.wait_ge(at_ready, n + 1)
                    down(0, parts[:-1])
                    turn(1)
                    down(0, parts[-1:])
                    pe.wait_ge(at_ready, n + 2)
                    down(1, parts).then_inc(slot_used, 1)

            pe.wait_ge(const_in, 16)
            for layer in range(DEPTH):
                if layer == 0:
                    c.hear(silu_c_ready)
                    modulation(0, COLUMN_TILES + GATE_TILES)
                to_features(xn, range(NB), xn_ready)
                projections(layer)
                attention(layer)
                ssd(layer)
                hyena(layer)
                output(layer)
                if layer + 1 < DEPTH:
                    modulation(layer + 1, GATE_TILES)
                to_features(xn, blocks_out(layer), xn_ready)
                S.drained()
                V.drained()
                if layer == 0:
                    c.hear(o_free, 2)
                    ffn_job(0, 0, True)
                    ffn_job(1, 2, False)
                else:
                    route()
                    c.hear(o_free, 2)
                    gather(0)
                    pe.wait_ge(table_ready, 1)
                    by_size(pe, 0, lambda few: expert_job(0, False, True, few))
                    with pe.Fori(1, NE - 1) as e:
                        by_size(pe, e, lambda few: expert_job(e, True, True, few))
                    by_size(pe, NE - 1, lambda few: expert_job(NE - 1, True, False, few))
                    put_back(NE - 1)
                    with pe.Fori(0, NE) as e:
                        again, n = second_turn(pe, e)
                        with pe.If(again):
                            gather(n)
                            expert_job(n, False, False, False)
                            put_back(n)

        @block.sync
        def _(sp):
            c = Counts(sp, None)
            sp.sem_inc(slot_used, SLOTS)
            sp.dma_start(feat[:, :], A["feat"]).then_inc(feat_in, 16)
            sp.dma_start(const[:, :], A["const"]).then_inc(const_in, 16)

            def ffn_loads(J, wg, wu, wd):
                for s in range(STEPS):
                    gu, dn = slot_views(s % SLOTS)
                    i = s % SLOTS
                    sp.wait_ge(slot_used, J * STEPS + (s + 1))
                    u, lo = UNITS[s], sum(UNITS[0:s])
                    hi = lo + u
                    sp.dma_start(gu[:, :, 0, 0:u], wg[:, lo:hi].rearrange("(k p) f -> p k f", p=P)
                                 ).then_inc(slot_in[i], 16)
                    sp.dma_start(gu[:, :, 1, 0:u], wu[:, lo:hi].rearrange("(k p) f -> p k f", p=P)
                                 ).then_inc(slot_in[i], 16)
                    sp.dma_start(dn[:, 0:u // P, :], wd[lo:hi, :].rearrange("(f p) d -> p f d", p=P)
                                 ).then_inc(slot_in[i], 16)

            def gate_biases(layer):
                for i, wh in enumerate((2, 5)):
                    for x in range(gates[layer].shape[2]):
                        sp.dma_start(gates[layer][:, i, x, :],
                                     A["b_ada"][layer, wh * D:wh * D + D].partition_broadcast(P)).then_inc(b_in, 16)

            def mixer_parameters(layer):
                sp.dma_start(fconst, A["filter_const"]).then_inc(filt_in, 16)
                sp.dma_start(fw1, A["hy_w1"][layer]).then_inc(filt_in, 16)
                sp.dma_start(fw2, A["hy_w2"][layer]).then_inc(filt_in, 16)
                sp.dma_start(fw3, A["hy_w3"][layer]).then_inc(filt_in, 16)
                sp.dma_start(fbf, A["hy_bf"][:, 4 * layer:4 * layer + 4]).then_inc(filt_in, 16)
                sp.dma_start(params[:, :], A["params"][layer, :].partition_broadcast(P)).then_inc(par_in, 16)

            mixer_parameters(0)
            tile_no = [0]
            for layer in range(DEPTH):
                if layer > 0:
                    sp.wait_ge(slot_used, 2 * STEPS + SLOTS)
                todo = list(tiles(layer))
                for i, (src, n) in enumerate(todo):
                    g = tile_no[0]
                    tile_no[0] += 1
                    if g >= 2:
                        sp.wait_ge(*tile_done[g - 2])
                    sp.dma_start(tile_view(g % 2, n), src.rearrange("(k p) n -> p k n", p=P)
                                 ).then_inc(tile_in[g % 2], 16)
                    if g == 1:
                        sp.dma_start(x_v[:, 0:2, :], A["x"][0].rearrange("(b p) d -> p b d", p=P)).then_inc(x_in, 16)
                        sp.dma_start(x_v[:, 2:4, :], A["ctx"][0].rearrange("(b p) d -> p b d", p=P)
                                     ).then_inc(x_in, 16)
                        gate_biases(0)
                    if layer + 1 < DEPTH and i == len(todo) - 5:
                        c.hear(y_ready)
                        mixer_parameters(layer + 1)
                    if layer + 1 < DEPTH and i == len(todo) - 3:
                        sp.wait_ge(x_ready, layer + 1)
                        gate_biases(layer + 1)
                sp.wait_ge(*tile_done[tile_no[0] - 1])
                if layer == 0:
                    for J in range(2):
                        ffn_loads(J, A["ffn_w_gate"][0], A["ffn_w_up"][0], A["ffn_w_down"][0])
                else:
                    sp.dma_start(router, A["moe_router"][0].rearrange("(k p) e -> p k e", p=P)
                                 ).then_inc(router_in, 16)
                    def expert_loads(j, e):
                        ffn_loads(j + 2, *[A[w][0][bass.ds(e, 1)].rearrange("a d f -> (a d) f")
                                           for w in ("moe_w_gate", "moe_w_up", "moe_w_down")])
                    with sp.Fori(0, NE) as e:
                        expert_loads(e, e)
                    sp.wait_ge(table_ready, 1)
                    with sp.Fori(0, NE) as e:
                        again, n = second_turn(sp, e)
                        with sp.If(again):
                            expert_loads(n, e)
            c.hear(layer_done, DEPTH)
            sp.dma_start(out[0].rearrange("(b p) d -> p b d", p=P), x_v[:, 0:2, :]).then_inc(out_done, 16)
            sp.wait_ge(out_done, 16)

        @block.gpsimd
        def _(pool):
            c = Counts(pool, pool_own)
            c.tell(nc.gpsimd.memset(silu_c, 0.0), zeros_ready)
            c.link(nc.gpsimd.memset(mhalf, -0.5))

            def rsqrt(o, i, w):
                c.hear(pow_asked)
                c.tell(nc.gpsimd.tensor_tensor(o, i, w, ALU.pow), pow_ready)

            for layer in range(DEPTH):
                nb = len(blocks_out(layer))
                if layer > 0:
                    c.hear(layer_done)
                nc.gpsimd.memset(xbcp[:, :, :, 0:1], 0.0)
                nc.gpsimd.memset(xbcp[:, :, :, SEQ + 1:SEQ + 2], 0.0)
                nc.gpsimd.memset(hyp[:, :, :, 0:1], 0.0)
                c.tell(nc.gpsimd.memset(hyp[:, :, :, SEQ + 1:SEQ + 2], 0.0), pads_ready)
                h40 = mhalf[:, 0:40].rearrange("p (b h) -> p b h", b=NB)
                rsqrt(srst[:, 0:NB], ssum[:, 0:NB], mhalf[:, 0:NB])
                rsqrt(qrst[:, 0:nb, :], qsum[:, 0:nb, :], h40[:, 0:nb, :])
                if nb < NB:
                    rsqrt(qrst[:, nb:NB, 8:10], qsum[:, nb:NB, 8:10], h40[:, nb:NB, 8:10])
                rsqrt(srst[:, 0:nb], ssum[:, 0:nb], mhalf[:, 0:nb])
                rsqrt(srst[:, 0:nb], ssum[:, 0:nb], mhalf[:, 0:nb])
                h16 = mhalf[:, 0:16].rearrange("p (b h) -> p b h", b=NB)
                rsqrt(grst[:, 0:nb, :], gs[:, 0:nb, :], h16[:, 0:nb, :])
                rsqrt(srst[:, 0:nb], ssum[:, 0:nb], mhalf[:, 0:nb])

        @block.scalar
        def _(act):
            c = Counts(act, act_own)
            S = Ring(c, A_BANKS, a_full, a_free)

            def f(o, i, func, **kw):
                return nc.scalar.activation(o, i, func, **kw)

            def take_copy(o, view=lambda b: b[:, :]):
                b = S.take()
                S.give(f(o, view(b), ACT.Copy))

            def norm(layer, blocks, wh, first):
                if not first:
                    c.hear(x_ready)
                elif layer == 0:
                    act.wait_ge(x_in, 32)
                else:
                    c.hear(layer_done)
                for b in blocks:
                    c.tell(f(junk, x_v[:, b, :], ACT.Square, accum_out=ssum[:, b:b + 1]), sq_ready)
                    c.done()
                if wh == 0:
                    c.hear(coef_ready)
                coef = coefs[layer]
                for b in blocks:
                    o = S.take()
                    s = b // 2
                    for k in range(4):
                        last = f(ht[:, k, b * P:b * P + P], o[:, k * P:k * P + P], ACT.Identity,
                                 scale=coef[:, wh + 1, k, s:s + 1], bias=coef[:, wh, k, s:s + 1])
                    S.give(last)

            def filter_stage(stage):
                if stage < 2:
                    c.hear(arg_ready)
                    c.tell(f(fh[stage], farg, ACT.Sin), sin_ready)
                if stage == 3:
                    for r in range(2):
                        for m in range(2):
                            take_copy(spec[:, r, m, :])

            ada_no = [0]

            def take_ada():
                take_copy(ada[:, ada_no[0] % 2, :])
                ada_no[0] += 1

            def seqs(b):
                return b[:, :].rearrange("p (s t) -> p s t", s=2)

            def attention(layer):
                for b in blocks_out(layer):
                    take_copy(qt[:, :, b * P:b * P + P], lambda o: o[:, :].rearrange("p (j t) -> p j t", j=4))
                us = units(layer)
                for i in range(len(us) + 1):
                    for n, t in enumerate(COLUMN_TILES if layer + 1 < DEPTH else []):
                        if i == ADA_EVERY * (n + 1):
                            take_ada()
                    if i < len(us):
                        b, h = us[i]
                        lo, hi = keys_of(b)
                        c.hear(sc_ready)
                        c.tell(f(pr[:, i % 2, 0:hi - lo], sc[:, i % 2, 0:hi - lo], ACT.Exp,
                                 bias=negm[:, b % 2, h:h + 1], accum_out=psumr[:, b % 2, h:h + 1]), p_ready)
                    if i >= 1:
                        b, h = us[i - 1]
                        lo, hi = keys_of(b)
                        take_copy(pt[:, (i - 1) % 2, 0:hi - lo], lambda o: o[:, 0:hi - lo])
                    for b in blocks_out(layer):
                        if i == min(8 * b + 10, len(us)):
                            c.hear(act_asked)
                            c.tell(f(snk, snk, ACT.Exp), act_did)

            def ssd(layer):
                for b in blocks_out(layer):
                    c.tell(f(tokp[:, b, COL_Z:D], tokp[:, b, COL_Z:D], ACT.Silu), zs_ready)
                for b in range(NB):
                    take_copy(xsb[:, b, :], lambda o: o[:, 0:384])
                c.hear(act_asked)
                f(wend, wend, ACT.Exp)
                c.tell(f(ela, la, ACT.Exp), act_did)
                for b in blocks_out(layer):
                    for r in range(2):
                        act.wait_ge(v_free, marks["seg", layer, b, r])
                        c.tell(f(decay[:, r, :, :], decay[:, r, :, :], ACT.Exp), dec_ready)

            def hyena(layer):
                ns = seqs_out(layer)
                nb, n = 2 * ns, SEQ * ns
                for ch in range(6):
                    take_copy(hyu[:, 0:nb, ch * P:ch * P + P],
                              lambda o: o[:, 0:nb * P].rearrange("p (b d) -> p b d", b=nb))
                for order in range(2):
                    for m in range(2):
                        take_copy(ur[:, m, 0:n], lambda o: o[:, 0:n])
                        take_copy(ui[:, m, 0:n], lambda o: o[:, 0:n])

            def ffn_job(J):
                for s in range(STEPS):
                    n = (J * STEPS + s) * 2
                    for b in range(2):
                        act.wait_ge(gu_full, n + b + 1)
                        u = UNITS[s]
                        f(sg[b][:, 0:u], bank[4 + b][:, 0:u], ACT.Silu).then_inc(sg_ready, 1)
                        act.wait_ge(t_full, n + b + 1)
                        f(at[b][:, 0:u // P, :], bank[6 + b][:, 0:u].rearrange("p (f t) -> p f t", t=P), ACT.Copy
                          ).then_inc(at_ready, 1)

            def take_gathered(j):
                for i in range(2):
                    act.wait_ge(xe_full, j * 2 + (i + 1))
                    f(xe[:, 4 * i:4 * i + 4, :], bank[5 + i][:, :].rearrange("p (k r) -> p k r", k=4), ACT.Copy
                      ).then_inc(xe_ready, 1)

            def take_turned(j):
                act.wait_ge(gt_full, j + 1)
                f(gt, bank[7][:, 0:2 * P], ACT.Copy).then_inc(gt_ready, 1)

            def expert_job(j, has_next, few):
                for s in range(STEPS):
                    act.wait_ge(gu_full, j * STEPS + (FFN_HALVES + s + 1))
                    rows, n = (64 * (UNITS[s] // P), P) if few else (P, UNITS[s])
                    f(sg[0][0:rows, 0:n], bank[2 + s % 2][0:rows, 0:n], ACT.Silu).then_inc(sg_ready, 1)
                    if s == 2:
                        take_turned(j)
                    if s == STEPS - 1 and has_next:
                        take_gathered(j + 1)
                    act.wait_ge(t_full, j * STEPS + (FFN_HALVES + s + 1))
                    if few:
                        f(at[0][:, 0, 0:rows], bank[4][:, 0:rows], ACT.Copy).then_inc(at_ready, 1)
                    else:
                        f(at[0][:, 0:n // P, :], bank[4][:, 0:n].rearrange("p (f t) -> p f t", t=P), ACT.Copy
                          ).then_inc(at_ready, 1)
                act.wait_ge(slot_used, j * STEPS + (3 * STEPS + SLOTS))
                rows = 64 if few else P
                f(ye[0:rows, 0:512], bank[0][0:rows, :], ACT.Copy).then_inc(ye_ready, 1)

            act.wait_ge(feat_in, 16)
            c.hear(zeros_ready)
            c.tell(f(silu_c[:, :, 0:2], feat[:, F_C:F_C + 16].rearrange("p (s k) -> p k s", s=2), ACT.Silu),
                   silu_c_ready)
            for layer in range(DEPTH):
                if layer == 0:
                    for n in range(len(COLUMN_TILES + GATE_TILES)):
                        take_ada()
                        if n in STAGE_AFTER_TILE:
                            filter_stage(STAGE_AFTER_TILE[n])
                norm(layer, range(NB), 0, True)
                for b in range(NB):
                    take_copy(tokp[:, b, 512:1024])
                for ch in range(4):
                    take_copy(xbcp[:, ch, :, 1:SEQ + 1], seqs)
                take_copy(dtu, lambda o: o[:, 0:32].rearrange("p (b h) -> p b h", b=NB))
                ns = seqs_out(layer)
                for ch in range(6):
                    take_copy(hyp[:, ch, 0:ns, 1:SEQ + 1], lambda o: seqs(o)[:, 0:ns, :])
                    if ch < 4:
                        c.hear(conv_ready)
                        c.tell(f(xbcs[:, ch, :], conv[:, ch % 2, :], ACT.Silu), xbc_ready)
                    if ch == 4:
                        c.hear(act_asked)
                        c.link(f(dte, dte, ACT.Exp))
                        f(dte, dte, ACT.Ln, bias=con("ones")[:, 0:1])
                        c.tell(f(aexp, par("ssd_a_log"), ACT.Exp), act_did)
                attention(layer)
                ssd(layer)
                hyena(layer)
                for b in blocks_out(layer):
                    take_copy(ht[:, 0:4, b * P:b * P + P], lambda o: o[:, :].rearrange("p (k t) -> p k t", k=4))
                if layer + 1 < DEPTH:
                    for stage in range(4):
                        filter_stage(stage)
                    for t in GATE_TILES:
                        take_ada()
                norm(layer, blocks_out(layer), 2, False)
                if layer == DEPTH - 1:
                    for b in range(2):
                        for half in range(2):
                            take_copy(h2[:, b, half * 512:half * 512 + 512])
                    c.hear(act_asked)
                    c.tell(f(top[:, 2, :], top[:, 2, :], ACT.Exp), act_did)
                if layer == 0:
                    for J in range(2):
                        ffn_job(J)
                else:
                    take_gathered(0)
                    act.wait_ge(table_ready, 1)
                    with act.Fori(0, NE - 1) as e:
                        by_size(act, e, lambda few: expert_job(e, True, few))
                    by_size(act, NE - 1, lambda few: expert_job(NE - 1, False, few))
                    with act.Fori(0, NE) as e:
                        again, n = second_turn(act, e)
                        with act.If(again):
                            take_gathered(n)
                            expert_job(n, False, False)

        @block.vector
        def _(dve):
            v = nc.vector
            c = Counts(dve, vec_own)
            V = Ring(c, V_BANKS, v_full, v_free)
            link = c.link

            def ask_rsqrt():
                c.hear(pow_ready)

            def mean_sq(o, n):
                c.tell(v.tensor_scalar(o, o, 1.0 / n, EPS, ALU.mult, ALU.add), pow_asked)

            def tt(o, a, b, op):
                return v.tensor_tensor(o, a, b, op)

            def filter_stage(layer, stage):
                if stage == 0:
                    dve.wait_ge(filt_in, 80 * (layer + 1))
                if stage < 2:
                    o = V.take()
                    V.give(v.tensor_scalar(farg, o[0:64, 0:SEQ], fbf[:, 2 * stage:2 * stage + 1],
                                           fbf[:, 2 * stage + 1:2 * stage + 2], ALU.add, ALU.mult))
                    c.done()
                    link(v.tensor_scalar(fk, farg, INV_2PI, ROUND, ALU.mult, ALU.add))
                    link(v.tensor_scalar(fk, fk, ROUND, None, ALU.subtract))
                    for part in TWO_PI:
                        link(v.scalar_tensor_tensor(out=farg, in0=fk, scalar=-part, in1=farg, op0=ALU.mult,
                                                    op1=ALU.add))
                    c.tell(v.tensor_scalar(farg, farg, PI_F, -PI_F, ALU.min, ALU.max), arg_ready)
                if stage == 2:
                    for t in range(2):
                        for d in range(2):
                            o = V.take()
                            dec = fcon(f"decay{d}").rearrange("p (t d) -> p t d", t=2)[:, t, :]
                            V.give(tt(fd[d].rearrange("p (o d) -> p o d", o=2),
                                      o[:, :].rearrange("p (o d) -> p o d", o=2), bc_in(dec, 2), ALU.mult))
                        c.done()
                        link(tt(fp[:, t, :], fd[0], fd[1], ALU.add))
                        ins = tt(fq[:, t, :], fd[0], fd[1], ALU.subtract)
                        if t == 0:
                            link(ins)
                        else:
                            c.tell(ins, fpq_ready)

            def ada_sums(layer, t):
                wh, half = t // 2, t % 2
                if t in COLUMN_TILES:
                    w = COEF_OF[wh]
                    f0 = layer * F_LAYER + F_BA + 8 * w + 4 * half
                    o = V.take()
                    V.give(tt(coefs[layer][:, w, 4 * half:4 * half + 4, :],
                              o[:, 0:8].rearrange("p (k s) -> p k s", s=2), bc(feat[:, f0:f0 + 4], 2), ALU.add))
                    return
                dve.wait_ge(b_in, 64 if layer == 0 else 96)
                for x in range(gates[layer].shape[2]):
                    g = gates[layer][:, (2, 5).index(wh), x, 512 * half:512 * half + 512]
                    o = V.take()
                    V.give(tt(g, o[:, :], g, ALU.add))

            def scales(layer):
                coef = coefs[layer]
                c.done()
                for w, norm_col in ((1, F_N1), (3, F_N2)):
                    f0 = layer * F_LAYER + norm_col
                    link(v.tensor_scalar(coef[:, w, :, :], coef[:, w, :, :], 1.0, None, ALU.add))
                    ins = tt(coef[:, w, :, :], coef[:, w, :, :], bc(feat[:, f0:f0 + KD], 2), ALU.mult)
                    if w == 1:
                        link(ins)
                    else:
                        c.tell(ins, coef_ready)
                        c.done()

            def norm(layer, blocks, wh):
                blocks = list(blocks)
                coef = coefs[layer]
                c.hear(sq_ready, len(blocks))
                mean_sq(ssum[:, 0:len(blocks)], D)
                ask_rsqrt()
                for b in blocks:
                    c.tell(v.tensor_scalar(xn[:, b, :], x_v[:, b, :], srst[:, b:b + 1], None, ALU.mult), xn_ready)
                for b in blocks:
                    o = V.take()
                    s = b // 2
                    for k in range(4):
                        last = v.tensor_scalar(ht[:, 4 + k, b * P:b * P + P], o[:, k * P:k * P + P],
                                               coef[:, wh + 1, 4 + k, s:s + 1], coef[:, wh, 4 + k, s:s + 1],
                                               ALU.mult, ALU.add)
                    V.give(last)

            def projections(layer):
                for b in blocks_out(layer):
                    o = V.take()
                    V.give(v.tensor_copy(tokp[:, b, 0:512], o[:, :]))

            def ssd_inputs(layer):
                c.hear(pads_ready)
                dve.wait_ge(a_free, marks["xbc", layer])
                for ch in range(4):
                    if ch >= 2:
                        c.hear(xbc_ready)
                    o = conv[:, ch % 2, :].rearrange("p (s t) -> p s t", s=2)
                    c.tell(convolve(o, xbcp[:, ch, :, :], 2, lambda i: fcol(layer, F_SW + 4 * i + ch),
                                    fcol(layer, F_SB + ch)), conv_ready)
                dve.wait_ge(a_free, marks["dt", layer])
                link(tt(dtu, dtu, bc_in(par("ssd_dt_bias"), NB), ALU.add))
                link(v.tensor_scalar(dte, dtu, -1.0, None, ALU.mult))
                c.tell(tt(dte, dtu, dte, ALU.min), act_asked)
                c.hear(act_did)
                c.hear(xbc_ready, 2)
                link(v.scalar_tensor_tensor(out=dt, in0=dtu, scalar=0.0, in1=dte, op0=ALU.max, op1=ALU.add))
                c.tell(v.scalar_tensor_tensor(out=dta, in0=dt, scalar=-1.0, in1=bc_in(aexp, NB), op0=ALU.mult,
                                              op1=ALU.mult), dta_ready)

            def attention(layer):
                dve.wait_ge(a_free, marks["kv", layer])
                dve.wait_ge(par_in, 16 * (layer + 1))
                c.done()
                link(v.tensor_scalar(qgain, par("q_norm"), HD ** -0.5, None, ALU.mult))
                nb = len(blocks_out(layer))

                def heads_of(b):
                    return 0 if b < nb else HEADS
                for b in range(NB):
                    h0 = heads_of(b)
                    src = tokp[:, b, h0 * HD:10 * HD]
                    link(tt(qn[:, h0 * HD:640], src, src, ALU.mult))
                    link(v.tensor_reduce(qsum[:, b, h0:10], qn[:, h0 * HD:640].rearrange("p (h d) -> p h d", d=HD),
                                         AX_X, ALU.add))
                mean_sq(qsum[:, 0:nb, :], HD)
                if nb < NB:
                    mean_sq(qsum[:, nb:NB, 8:10], HD)
                    ask_rsqrt()
                ask_rsqrt()
                for b in range(NB):
                    h0 = heads_of(b)
                    if b == 2:
                        ssd_inputs(layer)
                    if b >= 2:
                        dve.wait_ge(v_full, marks["turned", layer, b - 2])
                    dst = qn if b < 2 else qr[:, b % 2, :]
                    if h0 == 0:
                        q = tokp[:, b, 0:512].rearrange("p (g j d) -> p g j d", g=2, d=HD)
                        link(tt(dst[:, 0:512].rearrange("p (j g d) -> p g j d", g=2, d=HD), q,
                                bc(qrst[:, b, 0:8].rearrange("p (g j) -> p g j", g=2), HD), ALU.mult))
                        q = dst[:, 0:512].rearrange("p (h d) -> p h d", d=HD)
                        link(tt(q, q, bc_in(qgain, 8), ALU.mult))
                    k = dst[:, 512:640].rearrange("p (h d) -> p h d", d=HD)
                    link(tt(k, tokp[:, b, 512:640].rearrange("p (h d) -> p h d", d=HD),
                            bc(qrst[:, b, 8:10], HD), ALU.mult))
                    ins = tt(k, k, bc_in(par("k_norm"), 2), ALU.mult)
                    if b >= 2:
                        c.tell(ins, qr_ready)
                        continue
                    link(ins)

                    def halves(x):
                        x = x.rearrange("p (h a w f) -> p h a w f", a=2, w=2, f=16)
                        return x[:, :, :, 0, :], x[:, :, :, 1, :]
                    x1, x2 = halves(qn)
                    o1, o2 = halves(qr[:, b % 2, :])
                    cs, sn = [bc_in(con(w)[:, 32 * b:32 * b + 32].rearrange("p (a f) -> p a f", a=2), 10)
                              for w in ("cos", "sin")]
                    ra, rb = [x.rearrange("p (h a f) -> p h a f", a=2, f=16) for x in (rope_a, rope_b)]
                    tt(ra, x1, cs, ALU.mult)
                    link(tt(rb, x2, sn, ALU.mult))
                    link(tt(o1, ra, rb, ALU.subtract))
                    tt(ra, x1, sn, ALU.mult)
                    link(tt(rb, x2, cs, ALU.mult))
                    c.tell(tt(o2, ra, rb, ALU.add), qr_ready)
                for b in range(NB):
                    o = V.take()
                    V.give(v.tensor_copy(kt[:, b * P:b * P + P], o[:, 0:P]))
                c.done()
                us = units(layer)
                for i in range(len(us) + 1):
                    for n, t in enumerate(COLUMN_TILES if layer + 1 < DEPTH else []):
                        if i == ADA_EVERY * (n + 1) + 1:
                            ada_sums(layer + 1, t)
                            if n == len(COLUMN_TILES) - 1:
                                scales(layer + 1)
                    if i < len(us):
                        b, h = us[i]
                        lo, hi = keys_of(b)
                        o = V.take()
                        m0 = 512 * b if b < 2 else SEQ
                        V.give(v.tensor_tensor_reduce(out=sc[:, i % 2, 0:hi - lo], in0=o[:, 0:hi - lo],
                                                      in1=con("mask")[:, m0:m0 + hi - lo], scale=1.0, scalar=-3.0e38,
                                                      op0=ALU.add, op1=ALU.max, accum_out=rawm[:, b % 2, h:h + 1]))
                        c.done()
                        c.tell(v.tensor_scalar(negm[:, b % 2, h:h + 1], rawm[:, b % 2, h:h + 1],
                                               par("att_sinks")[:, h:h + 1], -1.0, ALU.max, ALU.mult), sc_ready)
                    for b in blocks_out(layer):
                        if i == min(8 * b + 10, len(us)):
                            c.done()
                            c.tell(tt(snk, negm[:, b % 2, :], par("att_sinks"), ALU.add), act_asked)
                            c.hear(act_did)
                            link(tt(rden, psumr[:, b % 2, :], snk, ALU.add))
                            link(v.reciprocal(rden, rden))
                            c.hear(o_full)
                            y = y_v[:, b, 0:ATT_W]
                            c.tell(tt(y.rearrange("p (h d) -> p h d", d=HD),
                                      O_BANKS[b % 2][:, :].rearrange("p (h d) -> p h d", d=HD),
                                      bc(rden, HD), ALU.mult), o_free)
                            c.done()
                            link(v.tensor_tensor_reduce(out=conv[:, 0, :], in0=y, in1=y, scale=1.0, scalar=0.0,
                                                        op0=ALU.mult, op1=ALU.add, accum_out=ssum[:, b:b + 1]))
                mean_sq(ssum[:, 0:nb], ATT_W)
                ask_rsqrt()
                for b in range(nb):
                    y = y_v[:, b, 0:ATT_W]
                    link(v.scalar_tensor_tensor(out=y, in0=y, scalar=srst[:, b:b + 1], in1=par("att_out_norm"),
                                                op0=ALU.mult, op1=ALU.mult))

            def convolve(o, x, n, w, bias):
                link(v.tensor_scalar(o, x[:, 0:n, 0:SEQ], w(0), bias, ALU.mult, ALU.add))
                link(v.scalar_tensor_tensor(out=o, in0=x[:, 0:n, 1:SEQ + 1], scalar=w(1), in1=o, op0=ALU.mult,
                                            op1=ALU.add))
                return v.scalar_tensor_tensor(out=o, in0=x[:, 0:n, 2:SEQ + 2], scalar=w(2), in1=o, op0=ALU.mult,
                                              op1=ALU.add)

            def fcol(layer, i):
                j = layer * F_LAYER + i
                return feat[:, j:j + 1]

            def ssd(layer):
                nb = len(blocks_out(layer))
                o = V.take()
                V.give(v.tensor_copy(la, o[:, 0:64].rearrange("p (b h) -> p b h", b=NB)))
                c.done()
                c.tell(tt(wend, la[:, :, 8:16], la[:, :, 0:8], ALU.subtract), act_asked)
                c.hear(act_did)
                link(tt(wend, wend, dt, ALU.mult))
                dve.wait_ge(a_free, marks["xsb", layer])
                for b in range(NB):
                    x = xsb[:, b, 0:256].rearrange("p (h d) -> p h d", d=HD)
                    for r in range(2):
                        last = tt(xw[:, r, :].rearrange("p (h d) -> p h d", d=HD), x,
                                  bc(wend[:, b, 4 * r:4 * r + 4], HD), ALU.mult)
                    c.tell(last, xw_ready)
                    o = V.take()
                    to = [(r, NEXT[r][b]) for r in range(2) if b in NEXT[r]]
                    for r, nxt in to:
                        last = v.tensor_copy(hin[:, r, nxt, :], o[:, 256 * r:256 * r + 256])
                    V.give(last)
                c.done()
                for i, (r, b) in enumerate(((0, 3), (0, 0), (1, 2), (1, 1))):
                    nxt = NEXT[r][b]
                    link(tt(ssdt[:, 0, :].rearrange("p (h d) -> p h d", d=HD),
                            hin[:, r, b, :].rearrange("p (h d) -> p h d", d=HD),
                            bc(ela[:, b, 8 + 4 * r:12 + 4 * r], HD), ALU.mult))
                    ins = tt(hin[:, r, nxt, :], hin[:, r, nxt, :], ssdt[:, 0, :], ALU.add)
                    if i < 3:
                        link(ins)
                    else:
                        c.tell(ins, h_ready)
                c.hear(zs_ready, nb)
                for b in blocks_out(layer):
                    for r, neg in enumerate(("neg_f", "neg_r")):
                        o = V.take()
                        for h in range(SSD_H):
                            last = v.scalar_tensor_tensor(out=decay[:, r, h, :], in0=o[:, h * P:h * P + P],
                                                          scalar=la[:, b, 4 * r + h:4 * r + h + 1], in1=con(neg),
                                                          op0=ALU.subtract, op1=ALU.add)
                        V.give(last)
                    c.hear(dec_ready, 2)
                    for h in range(SSD_H):
                        last = v.tensor_scalar(mix[:, h, :], decay[:, 0, h, :], dt[:, b, h:h + 1], None, ALU.mult)
                    link(last)
                    for h in range(SSD_H):
                        last = v.scalar_tensor_tensor(out=mix[:, h, :], in0=decay[:, 1, h, :],
                                                      scalar=dt[:, b, 4 + h:5 + h], in1=mix[:, h, :],
                                                      op0=ALU.mult, op1=ALU.add)
                    link(last)
                    for g in range(2):
                        o = V.take()
                        V.give(tt(mix[:, 2 * g:2 * g + 2, :], mix[:, 2 * g:2 * g + 2, :], bc_in(o[:, 0:P], 2),
                                  ALU.mult))
                    rs = [r for r in range(2) if FIRST[r] != b]
                    st = WORK[:, 4096:4608].rearrange("p (r h d) -> p r h d", r=2, d=HD)
                    for g in range(2):
                        o = V.take()
                        for r in rs:
                            last = tt(st[:, r, 2 * g:2 * g + 2, :],
                                      o[:, r * P:r * P + P].rearrange("p (h d) -> p h d", d=HD),
                                      bc(ela[:, b, 4 * r + 2 * g:4 * r + 2 * g + 2], HD), ALU.mult)
                        V.give(last)
                    y = y_v[:, b, ATT_W:ATT_W + SSD_W]
                    y4 = y.rearrange("p (h d) -> p h d", d=HD)
                    link(tt(y4, xsb[:, b, 0:256].rearrange("p (h d) -> p h d", d=HD), bc(par("ssd_d"), HD), ALU.mult))
                    for r in rs:
                        link(tt(y4, y4, st[:, r, :, :], ALU.add))
                    o = V.take()
                    V.give(tt(y, y, o[:, 0:256], ALU.add))
                    c.done()
                    link(tt(y, y, tokp[:, b, COL_Z:D], ALU.mult))
                    link(v.tensor_tensor_reduce(out=conv[:, 0, 0:256], in0=y, in1=y, scale=1.0, scalar=0.0,
                                                op0=ALU.mult, op1=ALU.add, accum_out=ssum[:, b:b + 1]))
                mean_sq(ssum[:, 0:nb], SSD_W)
                ask_rsqrt()
                for b in range(nb):
                    y = y_v[:, b, ATT_W:ATT_W + SSD_W]
                    link(v.scalar_tensor_tensor(out=y, in0=y, scalar=srst[:, b:b + 1], in1=par("ssd_norm"),
                                                op0=ALU.mult, op1=ALU.mult))

            def hyena(layer):
                ns = seqs_out(layer)
                nb, n = 2 * ns, SEQ * ns
                dve.wait_ge(a_free, marks["hy", layer])
                for ch in range(6):
                    if ch >= 2:
                        dve.wait_ge(a_full, marks["hturned", layer, ch - 2])
                    o = conv[:, ch % 2, 0:n].rearrange("p (s t) -> p s t", s=ns)
                    c.tell(convolve(o, hyp[:, ch, :, :], ns, lambda i: fcol(layer, F_HW + 6 * i + ch),
                                    fcol(layer, F_HB + ch)), hconv_ready)
                hyu_st = hyu.rearrange("p (s t) d -> p s t d", t=2)
                y_st = y_v.rearrange("p (s t) d -> p s t d", t=2)

                def s2(x):
                    return x.rearrange("p (s d) -> p s d", s=ns)

                ta, tb = s2(conv[:, 0, 0:n]), s2(conv[:, 1, 0:n])
                for order in range(2):
                    for m in range(2):
                        dve.wait_ge(a_free, marks["dft", layer, order, m])
                        kr, ki = [bc_in(spec[:, w, m, 256 * order:256 * order + 256], ns) for w in range(2)]
                        u_r, u_i, y_r, y_i = [s2(x[:, m, 0:n]) for x in (ur, ui, yr, yi)]
                        tt(ta, u_r, kr, ALU.mult)
                        link(tt(tb, u_i, ki, ALU.mult))
                        link(tt(y_r, ta, tb, ALU.subtract))
                        tt(ta, u_r, ki, ALU.mult)
                        link(tt(tb, u_i, kr, ALU.mult))
                        c.tell(tt(y_i, ta, tb, ALU.add), yspec_ready)
                        c.done()
                    bias = bc_in(par("hy_bias")[:, 256 * order:256 * order + 256], ns)
                    for t in range(2):
                        link(tt(ta, hyu_st[:, 0:ns, t, 0:256], bias, ALU.mult))
                        o = V.take()
                        V.give(tt(ta, ta, s2(o[:, 0:n]), ALU.add))
                        c.done()
                        x = hyu_st[:, 0:ns, t, 256 * (order + 1):256 * (order + 2)]
                        if order == 0:
                            c.tell(tt(hyu_st[:, 0:ns, t, 0:256], ta, x, ALU.mult), hz_ready)
                            c.done()
                        else:
                            link(tt(y_st[:, 0:ns, t, 768:1024], ta, x, ALU.mult))
                for b in range(nb):
                    y = y_v[:, b, 768:1024]
                    link(tt(conv[:, 0, 0:256], y, y, ALU.mult))
                    link(v.tensor_reduce(gs[:, b, :], conv[:, 0, 0:256].rearrange("p (g d) -> p g d", g=4), AX_X,
                                         ALU.add))
                mean_sq(gs[:, 0:nb, :], HY_W // HY_GROUPS)
                ask_rsqrt()
                for b in range(nb):
                    y = y_v[:, b, 768:1024]
                    y4 = y.rearrange("p (g d) -> p g d", g=4)
                    link(tt(y4, y4, bc(grst[:, b, :], HD), ALU.mult))
                    ins = tt(y, y, par("hy_out_norm"), ALU.mult)
                    if b < nb - 1:
                        link(ins)
                    else:
                        c.tell(ins, y_ready)

            def output(layer):
                for b in blocks_out(layer):
                    o = V.take()
                    V.give(v.tensor_copy(ht[:, 4:8, b * P:b * P + P], o[:, :].rearrange("p (k t) -> p k t", k=4)))
                for half in range(2):
                    for b in blocks_out(layer):
                        lo = half * 512
                        o = V.take()
                        V.give(tt(conv[:, 0, :], o[:, :], gates[layer][:, 0, b // 2, lo:lo + 512], ALU.mult))
                        c.done()
                        x = x_v[:, b, lo:lo + 512]
                        ins = tt(x, x, conv[:, 0, :], ALU.add)
                        if half == 1 and b == len(blocks_out(layer)) - 1:
                            c.tell(ins, x_ready)
                        else:
                            link(ins)
                        n = half * NB + b
                        if layer + 1 < DEPTH and n in STAGE_AFTER_PRODUCT:
                            filter_stage(layer + 1, STAGE_AFTER_PRODUCT[n])
                c.done()

            def route():
                o = V.take()
                V.give(v.tensor_copy(logit, o[:, 0:16].rearrange("p (b e) -> p b e", b=2)))
                c.done()
                rank = bc_in(con("rank8"), 2)
                for w in range(2):
                    mx, key = top[:, 2 * w, :], top[:, 2 * w + 1, :]
                    link(v.tensor_reduce(mx, logit, AX_X, ALU.max))
                    link(tt(eq, logit, bc(mx, NE), ALU.is_equal))
                    link(tt(eq, eq, rank, ALU.mult))
                    link(v.tensor_reduce(key, eq, AX_X, ALU.max))
                    link(tt(hot[:, w, :, :], eq, bc(key, NE), ALU.is_equal))
                    if w == 0:
                        link(v.scalar_tensor_tensor(out=logit, in0=hot[:, 0, :, :], scalar=-3.0e38, in1=logit,
                                                    op0=ALU.mult, op1=ALU.add))
                c.tell(tt(sel, hot[:, 0, :, :], hot[:, 1, :, :], ALU.add), sel_ready)
                c.tell(tt(top[:, 2, :], top[:, 2, :], top[:, 0, :], ALU.subtract), act_asked)
                c.hear(act_did)
                link(v.tensor_scalar(top[:, 3, :], top[:, 2, :], 1.0, None, ALU.add))
                link(v.reciprocal(top[:, 0, :], top[:, 3, :]))
                link(tt(top[:, 1, :], top[:, 2, :], top[:, 0, :], ALU.mult))
                link(tt(comb, hot[:, 0, :, :], bc(top[:, 0, :], NE), ALU.mult))
                link(tt(eq, hot[:, 1, :, :], bc(top[:, 1, :], NE), ALU.mult))
                link(tt(comb, comb, eq, ALU.add))
                o = V.take()
                far = 1.0e4
                link(v.tensor_scalar(pos, sel, -(1.0 + far), far, ALU.mult, ALU.add))
                link(tt(pos, pos, o[:, 0:16].rearrange("p (b e) -> p b e", b=2), ALU.add))
                link(v.tensor_scalar(few, o[:, 16:24], 64.5, None, ALU.is_lt))
                link(v.tensor_scalar(many, few, -1.0, 1.0, ALU.mult, ALU.add))
                V.give(v.tensor_scalar(over, o[:, 16:24], float(P), None, ALU.is_gt))
                c.done()

            def build_gather(j, e, shift):
                if isinstance(j, int) and j == 0:
                    pass
                else:
                    dve.wait_ge(gt_full, j)
                v.tensor_scalar(pe_col, pos[:, :, bass.ds(e, 1)].rearrange("p b e -> p (b e)"), shift, None, ALU.add
                                ).then_inc(col_ready, 1)
                dve.wait_ge(col_ready, j + 1)
                for b in range(2):
                    last = v.tensor_scalar(gm[:, b, :], con("iota"), pe_col[:, b:b + 1], None, ALU.is_equal)
                last.then_inc(g_ready, 1)

            def expert_job(j, e, has_last, has_next, few):
                for s in range(STEPS):
                    dve.wait_ge(sg_ready, j * STEPS + (FFN_HALVES + s + 1))
                    rows, n = (64 * (UNITS[s] // P), P) if few else (P, UNITS[s])
                    tt(av[0][0:rows, 0:n], sg[0][0:rows, 0:n], bank[2 + s % 2][0:rows, n:2 * n], ALU.mult
                       ).then_inc(a_ready, 1)
                    if s == 0 and has_last:
                        add_results(j, 1)
                    if s == 2:
                        v.tensor_copy(ce, comb[:, :, bass.ds(e, 1)].rearrange("p b e -> p (b e)")
                                      ).then_inc(ce_ready, 1)
                    if s == 3 and has_next:
                        build_gather(j + 1, e + 1, 0.0)
                if few:
                    v.memset(ye[64:P, :], 0.0)
                dve.wait_ge(slot_used, j * STEPS + (3 * STEPS + SLOTS))
                if few:
                    v.tensor_copy(ye[0:64, 512:1024], bank[1][64:P, :]).then_inc(ye_ready, 1)
                else:
                    v.tensor_copy(ye[:, 512:1024], bank[1][:, :]).then_inc(ye_ready, 1)

            def add_results(j, ago=0):
                dve.wait_ge(ce_ready, j + (1 - ago))
                dve.wait_ge(s_free, j * 4 + (1 - 4 * ago))
                for i in range(4):
                    dve.wait_ge(s_full, j * 4 + (i + 1 - 4 * ago))
                    y = y_v[:, i, 0:512]
                    v.scalar_tensor_tensor(out=y, in0=bank[5 + i % 3][:, :], scalar=ce[:, i // 2:i // 2 + 1],
                                           in1=y, op0=ALU.mult, op1=ALU.add).then_inc(s_free, 1)

            def gated(J):
                for s in range(STEPS):
                    n = (J * STEPS + s) * 2
                    for b in range(2):
                        dve.wait_ge(sg_ready, n + b + 1)
                        u = UNITS[s]
                        tt(av[b][:, 0:u], sg[b][:, 0:u], bank[4 + b][:, u:2 * u], ALU.mult).then_inc(a_ready, 1)

            for layer in range(DEPTH):
                if layer == 0:
                    dve.wait_ge(const_in, 16)
                    dve.wait_ge(feat_in, 16)
                    for n, t in enumerate(COLUMN_TILES):
                        ada_sums(0, t)
                        if n + 1 in STAGE_AFTER_TILE:
                            filter_stage(0, STAGE_AFTER_TILE[n + 1])
                    scales(0)
                    for t in GATE_TILES:
                        ada_sums(0, t)
                    dve.wait_ge(x_in, 32)
                norm(layer, range(NB), 0)
                projections(layer)
                attention(layer)
                ssd(layer)
                hyena(layer)
                output(layer)
                if layer + 1 < DEPTH:
                    for t in GATE_TILES:
                        ada_sums(layer + 1, t)
                norm(layer, blocks_out(layer), 2)
                if layer == 0:
                    for J in range(2):
                        gated(J)
                        dve.wait_ge(slot_used, (J + 1) * STEPS + SLOTS)
                        for i in range(4):
                            last = tt(y_v[:, i, 0:512], bank[i][:, :],
                                      gates[0][:, 1, J, 512 * (i % 2):512 * (i % 2) + 512], ALU.mult)
                        c.tell(last, sum_free)
                        c.done()
                        for i in range(4):
                            x = x_v[:, 2 * J + i // 2, 512 * (i % 2):512 * (i % 2) + 512]
                            last = tt(x, x, y_v[:, i, 0:512], ALU.add)
                        if J == 1:
                            c.tell(last, layer_done)
                            c.done()
                        else:
                            link(last)
                else:
                    route()
                    build_gather(0, 0, 0.0)
                    v.memset(y_v[:, :, 0:512], 0.0).then_inc(s_free, 1)
                    link(v.memset(before[:, 0:1], float(NE)))
                    for e in range(1, NE):
                        link(tt(before[:, e:e + 1], before[:, e - 1:e], over[:, e - 1:e], ALU.add))
                    tab = table[:, 0:4 * NE].rearrange("p (e w) -> p e w", w=4)
                    link(v.tensor_copy(tab[:, :, 0], over))
                    link(v.tensor_copy(tab[:, :, 2], few))
                    link(v.tensor_copy(tab[:, :, 3], many))
                    link(tt(pe_col[:, 0:1], before[:, NE - 1:NE], over[:, NE - 1:NE], ALU.add))
                    link(v.tensor_copy(table[:, 4 * NE:4 * NE + 1], pe_col[:, 0:1]))
                    c.tell(v.tensor_copy(tab[:, :, 1], before), table_ready)
                    c.done()
                    by_size(dve, 0, lambda few: expert_job(0, 0, False, True, few))
                    with dve.Fori(1, NE - 1) as e:
                        by_size(dve, e, lambda few: expert_job(e, e, True, True, few))
                    by_size(dve, NE - 1, lambda few: expert_job(NE - 1, NE - 1, True, False, few))
                    add_results(NE - 1)
                    with dve.Fori(0, NE) as e:
                        again, n = second_turn(dve, e)
                        with dve.If(again):
                            build_gather(n, e, -float(P))
                            expert_job(n, e, False, False, False)
                            add_results(n)
                    jobs = dve.value_load(table[0:1, 4 * NE:4 * NE + 1], min_val=NE, max_val=2 * NE)
                    dve.wait_ge(s_free, jobs * 4 + 1)
                    for i in range(4):
                        last = tt(y_v[:, i, 0:512], y_v[:, i, 0:512],
                                  gates[1][:, 1, 0, 512 * (i % 2):512 * (i % 2) + 512], ALU.mult)
                    link(last)
                    for i in range(4):
                        x = x_v[:, i // 2, 512 * (i % 2):512 * (i % 2) + 512]
                        last = tt(x, x, y_v[:, i, 0:512], ALU.add)
                    c.tell(last, layer_done)


INV_2PI = 1.0 / (2.0 * math.pi)
ROUND = 1.5 * 2.0 ** 23
TWO_PI = (6.28125, 2.0 * math.pi - 6.28125)
PI_F = 3.1415925


_BIG = ["x", "ctx", "w_ada", "b_ada", "w_in", "w_out", "hy_w1", "hy_w2", "hy_w3", "ffn_w_gate", "ffn_w_up",
        "ffn_w_down", "moe_router", "moe_w_gate", "moe_w_up", "moe_w_down"]


def constants():
    import numpy as np
    c = np.zeros((P, CON_COLS), np.float32)
    filt = np.zeros((P, FILT_COLS), np.float32)

    def put(name, a):
        a = np.asarray(a, np.float64).astype(np.float32)
        to, lo = (c, CON[name][0]) if name in CON else (filt, FILT[name][0])
        to[0:a.shape[0], lo:lo + a.shape[1]] = a

    i, j = np.arange(P)[:, None], np.arange(P)[None, :]
    put("ident", i == j)
    put("tri_f", i <= j)
    put("tri_r", i >= j)
    put("neg_f", np.where(i <= j, 0.0, NEG))
    put("neg_r", np.where(i >= j, 0.0, NEG))
    k = np.arange(SEQ)[None, :]
    z = np.zeros((P, SEQ))
    put("mask", np.concatenate([np.where(abs(k - i) <= WINDOW, 0.0, NEG), z,
                                np.where(abs(k - i - P) <= WINDOW, 0.0, NEG), z], axis=1))
    f32 = np.float32
    inv = (f32(10000.0) ** (-np.arange(0, 32, 2, dtype=f32) / f32(32))).astype(f32)
    t = np.arange(SEQ)
    ang = np.stack([(t // 64).astype(f32)[:, None] * inv, (t % 64).astype(f32)[:, None] * inv], axis=1)
    for name, fn in (("cos", np.cos), ("sin", np.sin)):
        put(name, fn(ang.astype(np.float64)).reshape(2, P, 32).transpose(1, 0, 2).reshape(P, 64))
    m, f = np.arange(SEQ)[:, None], np.arange(SEQ)[None, :]
    theta = math.pi * ((2 * f + 1) * m % (4 * SEQ)) / (2 * SEQ)

    def chunks(a):
        return a.reshape(2, P, -1).transpose(1, 0, 2).reshape(P, -1)
    put("dft_c", chunks(np.cos(theta)))
    put("dft_s", chunks(np.sin(theta)))
    put("inv_c", chunks(np.cos(theta).T / SEQ))
    put("inv_s", chunks(np.sin(theta).T / SEQ))
    tl = np.linspace(0.0, 1.0, SEQ)[:, None]
    deltas = abs(np.linspace(math.log(1e-2) / 1.5, math.log(1e-2) / 0.3, HY_W))
    dec = np.exp(-tl * deltas)
    put("decay0", chunks(dec))
    put("decay1", chunks(np.where(m == 0, 0.0, dec)))
    put("ones", np.ones((P, P)))
    put("iota", np.broadcast_to(np.arange(P), (P, P)))
    put("rank8", np.broadcast_to(NE - np.arange(NE), (P, NE)))
    w = (2.0 * math.pi / SEQ) * np.arange(SEQ)[:, None]
    freqs = np.linspace(1e-4, 15, 16)[None, :]
    put("pos", np.concatenate([tl, np.cos(freqs * w), -np.sin(freqs * w)], axis=1).T)
    put("gsel", np.concatenate([np.broadcast_to(i % 32 == s, (P, P)) for s in range(2)], axis=1))
    return c, filt


def kernel(**inputs):
    import numpy as np
    import concourse.bacc as bacc
    from concourse.bass_utils import run_bass_kernel_spmd

    a = {k: np.ascontiguousarray(v) for k, v in inputs.items()}
    cols = []
    for l in range(DEPTH):
        cols += [a["norm1"][l].reshape(8, P), a["norm2"][l].reshape(8, P), a["ssd_conv_w"][l].reshape(12, P),
                 a["ssd_conv_b"][l].reshape(4, P), a["hy_conv_w"][l].reshape(18, P), a["hy_conv_b"][l].reshape(6, P),
                 a["b_ada"][l].reshape(6, 8, P)[[0, 1, 3, 4]].reshape(32, P)]
    cols += [a["c"].reshape(8, P), a["c_ctx"].reshape(8, P)]
    data = {n: a[n] for n in _BIG}
    data["feat"] = np.ascontiguousarray(np.concatenate(cols, axis=0).T)
    data["params"] = np.concatenate([a[n].reshape(DEPTH, -1) for n, _ in PARTS], axis=1)
    data["hy_bf"] = np.ascontiguousarray(np.concatenate(
        [a[n][l][:, None] for l in range(DEPTH) for n in ("hy_b1", "hy_f1", "hy_b2", "hy_f2")], axis=1))
    data["const"], data["filter_const"] = constants()

    nc = bacc.Bacc("TRN2", target_bir_lowering=False, num_devices=1)
    arrays, views = {}, {}
    for name, v in data.items():
        arrays[f"in_{name}"] = v
        views[name] = nc.dram_tensor(f"in_{name}", v.shape, mybir.dt.from_np(v.dtype), kind="ExternalInput").ap()
    out = nc.dram_tensor("out_x", (1, SEQ, D), F32, kind="ExternalOutput").ap()
    hybrid_block(nc, views, out)
    r = run_bass_kernel_spmd(nc, [arrays], core_ids=[0])
    return r.results[0]["out_x"]
```
